# Optimizing a Trainium2 kernel written in Bass

```python
import math
import jax
import jax.numpy as jnp
from jax import lax
import numpy as np

D_MODEL = 2048
BATCH = 1
SEQ = 256
DEPTH = 2

D_MIX = D_MODEL
GLA_HEADS = 4
GLA_DK = D_MIX // 16
GLA_DV = D_MIX // 8
GLA_GATE_RANK = 16
GLA_GATE_TAU = 16.0
GLA_CHUNK = 64
DSA_HEADS = 8
DSA_HEAD_DIM = 128
IDX_HEADS = 16
IDX_DIM = 64
DSA_TOPK_MAX = 256
DSA_Q_BLOCK = 64
ROPE_THETA = 500000.0
ROPE_FRACTION = 4
D_FF = 4 * D_MODEL
EPS = 1e-6
NEG_INF = -1e30

IN_SPLITS = (
    GLA_HEADS * GLA_DK,
    GLA_HEADS * GLA_DK,
    GLA_HEADS * GLA_DV,
    GLA_HEADS * GLA_DV,
    GLA_GATE_RANK,
    DSA_HEADS * DSA_HEAD_DIM,
    DSA_HEADS * DSA_HEAD_DIM,
    DSA_HEADS * DSA_HEAD_DIM,
    IDX_HEADS * IDX_DIM,
    IDX_DIM,
    IDX_HEADS,
)
D_IN = sum(IN_SPLITS)

kernel_name = "hybrid_gla_dsa_sandwich_trunk"

def rms_norm(x, g):
    xf = x.astype(jnp.float32)
    y = xf * lax.rsqrt(jnp.mean(xf * xf, axis=-1, keepdims=True) + EPS)
    return (y * g.astype(jnp.float32)).astype(x.dtype)

def rope_tables(positions, head_dim):
    r = head_dim // ROPE_FRACTION
    inv_freq = ROPE_THETA ** (-(jnp.arange(0, r, 2, dtype=jnp.float32) / r))
    ang = positions.astype(jnp.float32)[..., None] * inv_freq
    return jnp.cos(ang)[:, :, None, :], jnp.sin(ang)[:, :, None, :]

def apply_partial_rope(x, cos, sin):
    r = 2 * cos.shape[-1]
    xr = x[..., :r].astype(jnp.float32)
    x1, x2 = xr[..., : r // 2], xr[..., r // 2:]
    rot = jnp.concatenate([x1 * cos - x2 * sin, x2 * cos + x1 * sin], axis=-1)
    return jnp.concatenate([rot.astype(x.dtype), x[..., r:]], axis=-1)

def gla_chunked(q, k, v, log_a):
    B, S, H, DK = q.shape
    DV = v.shape[-1]
    C = GLA_CHUNK
    N = S // C

    def to_chunks(t):
        return t.reshape(B, N, C, H, t.shape[-1]).transpose(0, 3, 1, 2, 4).astype(jnp.float32)

    qc = to_chunks(q) * (DK ** -0.5)
    kc, vc, gc = to_chunks(k), to_chunks(v), to_chunks(log_a)
    b = jnp.cumsum(gc, axis=3)
    b_last = b[:, :, :, -1:, :]
    q_dec = qc * jnp.exp(b)
    k_inv = kc * jnp.exp(-b)
    k_dec = kc * jnp.exp(b_last - b)
    causal = jnp.tril(jnp.ones((C, C), dtype=bool))
    attn = jnp.where(causal, jnp.einsum('bhncd,bhnjd->bhncj', q_dec, k_inv), 0.0)
    o_intra = jnp.einsum('bhncj,bhnje->bhnce', attn, vc)
    d_state = jnp.einsum('bhncd,bhnce->bhnde', k_dec, vc)
    decay = jnp.exp(b_last[:, :, :, 0, :])

    def step(state, inp):
        dec, ds = inp
        return dec[..., None] * state + ds, state

    _, states = lax.scan(step, jnp.zeros((B, H, DK, DV), jnp.float32),
                         (decay.transpose(2, 0, 1, 3), d_state.transpose(2, 0, 1, 3, 4)))
    states = states.transpose(1, 2, 0, 3, 4)
    o = o_intra + jnp.einsum('bhncd,bhnde->bhnce', q_dec, states)
    return o.transpose(0, 2, 3, 1, 4).reshape(B, S, H, DV).astype(v.dtype)

def dsa_attention(q, k, v, iq, ik, iw):
    B, S, H, Dh = q.shape
    QB = DSA_Q_BLOCK
    NB = S // QB
    topk = min(DSA_TOPK_MAX, S // 4)
    key_pos = jnp.arange(S)
    iw = iw * (IDX_HEADS ** -0.5)

    def blocks(t):
        return t.reshape((B, NB, QB) + t.shape[2:]).swapaxes(0, 1)

    def one_block(args):
        qb, iqb, iwb, start = args
        qpos = start + jnp.arange(QB)
        logits = jnp.einsum('bqhd,bsd->bqsh', iqb, ik) * (IDX_DIM ** -0.5)
        score = jnp.einsum('bqsh,bqh->bqs', jax.nn.relu(logits), iwb).astype(jnp.float32)
        visible = key_pos[None, :] <= qpos[:, None]
        score = jnp.where(visible[None], score, NEG_INF)
        _, sel = lax.top_k(score, topk)
        k_sel = jax.vmap(lambda kb, ib: kb[ib])(k, sel)
        v_sel = jax.vmap(lambda vb, ib: vb[ib])(v, sel)
        s = jnp.einsum('bqhd,bqkhd->bqhk', qb, k_sel).astype(jnp.float32) * (Dh ** -0.5)
        valid = (sel <= qpos[None, :, None])[:, :, None, :]
        p = jax.nn.softmax(jnp.where(valid, s, NEG_INF), axis=-1)
        return jnp.einsum('bqhk,bqkhd->bqhd', p.astype(v.dtype), v_sel)

    starts = jnp.arange(NB, dtype=jnp.int32) * QB
    out = lax.map(one_block, (blocks(q), blocks(iq), blocks(iw), starts))
    return out.swapaxes(0, 1).reshape(B, S, H, Dh)

def hybrid_mixer(h, cos_a, sin_a, cos_i, sin_i, w_in, gla_wa2, gla_ba, gla_norm, w_out):
    B, S, _ = h.shape
    proj = h @ w_in
    points = np.cumsum(IN_SPLITS)[:-1].tolist()
    gq, gk, gv, gg, gr, dq, dk, dv, iq, ik, iw = jnp.split(proj, points, axis=-1)

    log_a = jax.nn.log_sigmoid((gr @ gla_wa2 + gla_ba).astype(jnp.float32)) / GLA_GATE_TAU
    o_gla = gla_chunked(gq.reshape(B, S, GLA_HEADS, GLA_DK), gk.reshape(B, S, GLA_HEADS, GLA_DK),
                        gv.reshape(B, S, GLA_HEADS, GLA_DV), log_a.reshape(B, S, GLA_HEADS, GLA_DK))
    o_gla = rms_norm(o_gla, gla_norm) * jax.nn.silu(gg.reshape(B, S, GLA_HEADS, GLA_DV))

    dq = apply_partial_rope(dq.reshape(B, S, DSA_HEADS, DSA_HEAD_DIM), cos_a, sin_a)
    dk = apply_partial_rope(dk.reshape(B, S, DSA_HEADS, DSA_HEAD_DIM), cos_a, sin_a)
    dv = dv.reshape(B, S, DSA_HEADS, DSA_HEAD_DIM)
    iq = apply_partial_rope(iq.reshape(B, S, IDX_HEADS, IDX_DIM), cos_i, sin_i)
    ik = apply_partial_rope(ik[:, :, None, :], cos_i, sin_i)[:, :, 0, :]
    o_dsa = dsa_attention(dq, dk, dv, iq, ik, iw)

    o = jnp.concatenate([o_gla.reshape(B, S, -1), o_dsa.reshape(B, S, -1)], axis=-1)
    return o @ w_out

def sq_relu_mlp(h, w_up, w_down):
    u = jax.nn.relu(h @ w_up)
    return (u * u) @ w_down

def setup_inputs(seed: int = 0) -> dict:
    key = jax.random.key(seed)
    ks = jax.random.split(key, 16)
    f32 = jnp.float32

    def gain(k, shape):
        return 1.0 + 0.02 * jax.random.normal(k, shape, f32)

    def dense(k, shape, fan_in):
        return jax.random.normal(k, shape, f32) * (fan_in ** -0.5)

    x = jax.random.normal(ks[0], (BATCH, SEQ, D_MODEL), f32)
    positions = jnp.broadcast_to(jnp.arange(SEQ, dtype=jnp.int32)[None, :], (BATCH, SEQ))
    return {
        "x": x,
        "positions": positions,
        "norm_mix_pre": gain(ks[1], (DEPTH, D_MODEL)),
        "w_in": dense(ks[2], (DEPTH, D_MODEL, D_IN), D_MODEL),
        "gla_wa2": dense(ks[3], (DEPTH, GLA_GATE_RANK, GLA_HEADS * GLA_DK), GLA_GATE_RANK),
        "gla_ba": 0.02 * jax.random.normal(ks[4], (DEPTH, GLA_HEADS * GLA_DK), f32),
        "gla_norm": gain(ks[5], (DEPTH, GLA_DV)),
        "w_out": dense(ks[6], (DEPTH, D_MIX, D_MODEL), D_MIX),
        "norm_mix_post": gain(ks[7], (DEPTH, D_MODEL)),
        "norm_ffn_pre": gain(ks[8], (DEPTH, D_MODEL)),
        "w_up": dense(ks[9], (DEPTH, D_MODEL, D_FF), D_MODEL),
        "w_down": dense(ks[10], (DEPTH, D_FF, D_MODEL), D_FF),
        "norm_ffn_post": gain(ks[11], (DEPTH, D_MODEL)),
    }

def reference(x, positions, norm_mix_pre, w_in, gla_wa2, gla_ba, gla_norm, w_out,
              norm_mix_post, norm_ffn_pre, w_up, w_down, norm_ffn_post):
    cos_a, sin_a = rope_tables(positions, DSA_HEAD_DIM)
    cos_i, sin_i = rope_tables(positions, IDX_DIM)
    h = x
    for l in range(DEPTH):
        m = hybrid_mixer(rms_norm(h, norm_mix_pre[l]), cos_a, sin_a, cos_i, sin_i,
                         w_in[l], gla_wa2[l], gla_ba[l], gla_norm[l], w_out[l])
        h = h + rms_norm(m, norm_mix_post[l])
        f = sq_relu_mlp(rms_norm(h, norm_ffn_pre[l]), w_up[l], w_down[l])
        h = h + rms_norm(f, norm_ffn_post[l])
    return h


_drawn_inputs = setup_inputs


def setup_inputs(seed=0):
    import zlib

    import numpy as np

    out = dict(_drawn_inputs(seed))
    spreads = {}
    factors = {'gla_ba': 4.254}
    for name, (base, spread) in spreads.items():
        noise = np.random.default_rng([zlib.crc32(name.encode()), seed]).standard_normal(out[name].shape)
        drawn = base * np.exp(spread * noise) if base else spread * noise
        out[name] = jnp.asarray(drawn.astype(out[name].dtype))
    for name, factor in factors.items():
        out[name] = (out[name] * factor).astype(out[name].dtype)
    return out
```

```python
from contextlib import ExitStack

import numpy as np

import concourse.bass as bass
from concourse import mybir
from concourse.alu_op_type import AluOpType as ALU

F32 = mybir.dt.float32
F32R = mybir.dt.float32r
I32 = mybir.dt.int32
ACT = mybir.ActivationFunctionType
AX_X = mybir.AxisListType.X

P = 128
SEQ, D, DEPTH, D_FF = 256, 2048, 2, 8192
TT = SEQ // P
KT = D // P
GH, DK, DV, RANK, TAU, CHUNK = 4, 128, 256, 16, 16.0, 64
NCH = SEQ // CHUNK
AH, DH = 8, 128
IH, DI = 16, 64
TOPK = min(256, SEQ // 4)
ROPE_THETA, ROPE_FRACTION = 500000.0, 4
EPS, NEG = 1e-6, -1e30
TAKEN = -3e38
SPLITS = dict(gq=GH * DK, gk=GH * DK, gv=GH * DV, gg=GH * DV, gr=RANK, dq=AH * DH, dk=AH * DH,
              dv=AH * DH, iq=IH * DI, ik=DI, iw=IH)
COL, _c = {}, 0
for _n, _w in SPLITS.items():
    COL[_n] = _c
    _c += _w
D_IN = _c

BLK = 1024
RAW, HIS, QB = 8, 4, 4
MISC_W = DI + IH
O_T, O_TOK, O_OUT, O_FFN = 1, 9, 15, 19
NQ, UP, DN = 4, 4, 4
OCTETS = O_FFN + NQ * (UP + DN)
T_COLS = ["iq", "dq", "dk", "gq"]
TOK_COLS = ["dv", "gv", "gg"]
QT = D_FF // NQ // P
T_IQ, T_DQ, T_DK, T_GQ, T_GK = 0, 8, 16, 24, 28

A_MISC, A_T, A_TOK, A_OUT, A_FFN = 0, 1, 9, 12, 14
PAIR_USES = A_FFN + NQ * (UP + DN // 2)

FILLS = [(name, i) for name, n in (
    ("norm1", 8), ("rb", 1), ("z", 2), ("iw", 1), ("log0", 4), ("log1", 8), ("sc0", 2), ("pt0", 2),
    ("sc1", 4), ("pv0", 2), ("pt1", 4), ("kd", 2), ("at", 1), ("pv1", 2), ("ds", 6), ("o", 4), ("ot", 4),
    ("norm2", 8)) for i in range(n)]
BANKS = 4
BANK, USES = {}, [0] * BANKS
for _i, _f in enumerate(FILLS):
    BANK[_f] = (_i % BANKS, USES[_i % BANKS])
    USES[_i % BANKS] += 1

PER = dict(gr_hi=1, gr_lo=1, ssq=10, ms=2, r0=5, rstd=2, y_hi=16, half=50, rot=52, scaled=1,
           zabs=1, zl=1, zsc=1, eb=1, enb=1, edin=1, edec=1, gla_q=1, gla_kinv=1, gla_k=1, relu_used=12,
           causal=2, masked=2, allowed=2, negmax=2, expd=2, probs=2, pv_hi=4,
           at_masked=2, ossq=4, gate_e=2, ot_hi=4, summed=32, squared=32, u_hi=32, u_lo=32,
           h_done=16, gains=1)
DVE_STEPS, ACT_STEPS = 94, 6
NORM = 8
S_PRE, S_OUT, S_PRE2, S_DOWN = 1, 2, 6, 7
OUT_ROWS = [8, 10, 12, 14, 0, 2, 4, 6]


def rope_constants():
    c = np.zeros((P, 4), np.float32)
    for col, dim in ((0, DH), (2, DI)):
        r = dim // ROPE_FRACTION
        inv = np.float32(ROPE_THETA) ** (-(np.arange(0, r, 2, dtype=np.float32) / np.float32(r)))
        for p in range(P):
            d = p % dim
            if d < r:
                c[p, col] = inv[d % (r // 2)]
                c[p, col + 1] = -1.0 if d < r // 2 else 1.0
    return c


def swap_mask(half):
    return [i + half if i < half else i - half if i < 2 * half else i for i in range(32)]


def trunk(nc, x, positions, norm_mix_pre, w_in, gla_wa2, gla_ba, gla_norm, w_out, norm_mix_post,
          norm_ffn_pre, w_up, w_down, norm_ffn_post, rope_c, out):
    with ExitStack() as ctx:
        top = [-(-nc.sbuf_base // 64) * 64]

        def place(name, shape, dt=F32, at=None):
            where = top[0] if at is None else at
            if at is None:
                top[0] += -(-int(np.prod(shape[1:])) * 4 // 32) * 32
            return nc.alloc_sbuf_tensor_at(name, shape, dt, offset=where)

        KB = 1024
        h = place("h", [P, TT, D])
        Y = top[0]
        y = place("y", [P, KT, 2 * SEQ], F32R)
        y_scr = place("y_scr", [P, TT, D], at=Y)
        LR = top[0]
        raw = place("raw_ring", [P, RAW, BLK])
        lo = place("lo_ring", [P, RAW, BLK], F32R, at=LR)
        hi = place("hi_ring", [P, HIS, BLK], F32R)
        U = top[0]
        u = place("u", [P, QT, 2 * SEQ], F32R)
        oT = place("oT", [P, KT, 2 * SEQ], F32R, at=U)
        probs = place("probs", [P, AH, SEQ], at=U)
        rb = place("rb", [P, SEQ], at=U)
        rot_k = place("rot_k", [P, 2, SEQ], at=U + 8 * KB)
        kinv = place("kinv", [P, GH, SEQ], at=U + 8 * KB)
        za = place("za", [P, GH, SEQ], at=U + 12 * KB)
        at_sb = place("at_sb", [P, TT, GH, CHUNK], at=U + 12 * KB)
        relus = place("relus", [P, BANKS, 2 * SEQ], at=U + 16 * KB)
        swapped = place("swapped", [P, 2, SEQ], at=U + 24 * KB)
        fresh = place("fresh", [P, 2, 2, SEQ], at=U + 26 * KB)
        FA = top[0]
        facc = place("facc", [P, TT, D])
        dv = place("dv", [P, TT, AH * DH], at=FA)
        gv = place("gv", [P, TT, GH * DV], at=FA + 8 * KB)
        TS = top[0]
        ts = place("ts", [P, 32, SEQ])
        ptT = place("ptT", [P, AH, TT, P], at=TS)
        states = place("states", [P, NCH - 1, GH, DV], at=TS + 8 * KB)
        kd = place("kd", [P, TT, GH * DK], at=TS + 20 * KB)
        gpost = place("gpost", [P, D], at=TS)
        u2 = place("u2", [P, 2, 2, SEQ], at=TS + 8 * KB)
        gains_in = place("gains_in", [P, P], at=TS)
        gg = place("gg", [P, TT, GH * DV])
        misc = place("misc", [P, SEQ])
        GR = top[0]
        gr = place("gr", [P, SEQ])
        w_gr = place("w_gr", [P, KT, RANK], at=GR)
        ikz = place("ikz", [P, 2, SEQ])
        rot_a = place("rot_a", [P, 2, SEQ])
        cos_a, sin_a = rot_a[:, 0, :], rot_a[:, 1, :]
        rot_i = place("rot_i", [P, 2, SEQ])
        cos_i, sin_i = rot_i[:, 0, :], rot_i[:, 1, :]
        ident = place("ident", [P, P])
        within = place("within", [P, SEQ])
        gains_all = place("gains_all", [P, DEPTH, 2 * KT + GH])
        gains = place("gains", [P, 2 * KT + GH])
        wa2 = place("wa2", [P, GH * DK])
        gnorm = place("gnorm", [P, DV])
        score = place("score", [P, TT, SEQ])
        scr = place("scr", [P, 2, 2, SEQ])
        ZB = top[0]
        zb = place("zb", [P, GH, SEQ])
        gr_hi = place("gr_hi", [P, KT, RANK], F32R, at=ZB)
        gr_lo = place("gr_lo", [P, KT, RANK], F32R, at=ZB + KB)
        iw = place("iw", [P, TT, IH])
        top8 = place("top8", [P, 8])
        decay = place("decay", [P, GH, NCH])
        stat = place("stat", [P, 6, 8])
        pre = place("pre", [P, 3, TT])
        smax = place("smax", [P, 3, AH])
        eps_c, one_c = place("eps_c", [P, 1]), place("one_c", [P, 1])
        rc = place("rc", [P, 4])
        assert top[0] <= nc.sbuf_usable_end, top[0] - nc.sbuf_usable_end
        scr_gate = place("scr_gate", [P, TT, 2, 512], at=U)
        pos_i = place("pos_i", [P, SEQ], I32, at=U)
        ang = [place(f"ang{i}", [P, SEQ], at=U + (1 + i) * KB) for i in range(6)]

        acc = ctx.enter_context(nc.psum_tensor("acc", [P, 4, 512], F32))
        work = ctx.enter_context(nc.psum_tensor("work", [P, BANKS, 512], F32))

        def sem(name):
            return ctx.enter_context(nc.semaphore(name))

        landed = [sem(f"landed{i}") for i in range(RAW)]
        block_done = sem("block_done")
        hi_done, lo_done = sem("hi_done"), sem("lo_done")
        acc_free = [sem(f"acc_free{i}") for i in range(2)]
        bank_ready = [sem(f"bank_ready{i}") for i in range(BANKS)]
        bank_free = [sem(f"bank_free{i}") for i in range(BANKS)]
        S = {n: sem("s_" + n) for n in PER}
        wa2_in, gnorm_in, gpost_in, w_gr_in = (sem(n) for n in ("wa2_in", "gnorm_in", "gpost_in", "w_gr_in"))
        dve_step, act_step = sem("dve_step"), sem("act_step")
        weighed = sem("weighed")
        dve_stood, pool_stood, pe_stood = sem("dve_stood"), sem("pool_stood"), sem("pe_stood")
        setup_dma, rope_in, set_pool, consts, set_dve, set_act, set_pe, stored = (sem(n) for n in (
            "setup_dma", "rope_in", "set_pool", "consts", "set_dve", "set_act", "set_pe", "stored"))
        SETUP_DMAS, CONSTS = 1 + 3 * DEPTH, 5
        NG = 2 * KT + GH

        w_in_v = w_in.rearrange("l (k p) c -> p l k c", p=P)
        w_out_v = w_out.rearrange("l (k p) c -> p l k c", p=P)
        w_up_v = w_up.rearrange("l (k p) c -> p l k c", p=P)
        w_dn_v = w_down.rearrange("l (k p) c -> p l k c", p=P)

        def done(number):
            return number + (1 + RAW)

        block = ctx.enter_context(nc.Block())

        @block.sync
        def _(sp):
            def load(slot, number, src, k, c):
                sp.wait_ge(block_done, number + 1)
                sp.dma_start(raw[:, slot, 0:k * c].rearrange("p (k c) -> p k c", k=k),
                             src.rearrange("p l k c -> p (l k) c")).then_inc(landed[slot], 16)

            def misc_quad(L, number, half):
                w = MISC_W if half else 512
                for j in range(half * QB, half * QB + QB):
                    load(j, number + j, w_in_v[:, bass.ds(L, 1), 2 * j:2 * j + 2, D_IN - w:D_IN], 2, w)

            def feature_octet(L, number, w, col):
                for j in range(RAW):
                    half, b = j // QB, j % QB
                    load(j, number + j, w[:, bass.ds(L, 1), 4 * b:4 * b + 4, bass.ds(col + 256 * half, 256)], 4, 256)

            def token_octet(L, number, w, rows, col):
                for j in range(RAW):
                    load(j, number + j, w[:, bass.ds(L, 1), bass.ds(rows[j], 2), bass.ds(col, 512)], 2, 512)

            for l in range(DEPTH):
                for row, src, n in ((0, norm_mix_pre, KT), (KT, norm_ffn_pre, KT), (2 * KT, gla_ba, GH)):
                    sp.dma_start(gains_in[l * NG + row:l * NG + row + n, :],
                                 src[l].rearrange("(k p) -> k p", p=P)).then_inc(setup_dma, 16)
            sp.dma_start(h[:], x[0].rearrange("(t p) d -> p t d", p=P)).then_inc(setup_dma, 16)
            straight = [2 * b for b in range(RAW)]
            misc_quad(0, 0, 0)
            with sp.Fori(0, DEPTH) as L:
                n0 = L * (8 * OCTETS)
                sp.dma_start(w_gr[:], w_in_v[:, bass.ds(L, 1), :, COL["gr"]:COL["gr"] + RANK]
                             .rearrange("p l k c -> p (l k) c")).then_inc(w_gr_in, 16)
                misc_quad(L, n0, 1)
                for g, name in enumerate(T_COLS):
                    with sp.Fori(0, 2) as i:
                        feature_octet(L, n0 + i * 8 + 8 * (O_T + 2 * g), w_in_v, i * 512 + COL[name])
                for g, name in enumerate(TOK_COLS):
                    with sp.Fori(0, 2) as i:
                        token_octet(L, n0 + i * 8 + 8 * (O_TOK + 2 * g), w_in_v, straight, i * 512 + COL[name])
                with sp.Fori(0, 4) as i:
                    token_octet(L, n0 + i * 8 + 8 * O_OUT, w_out_v, OUT_ROWS, i * 512)
                with sp.Fori(0, NQ) as q:
                    nq = n0 + q * (8 * (UP + DN)) + 8 * O_FFN
                    with sp.Fori(0, UP) as i:
                        feature_octet(L, nq + i * 8, w_up_v, q * (QT * P) + i * 512)
                    with sp.Fori(0, DN) as i:
                        token_octet(L, nq + i * 8 + 8 * UP, w_dn_v, [q * QT + 2 * b for b in range(RAW)], i * 512)
                misc_quad(L * -1 + (DEPTH - 1), n0 + 8 * OCTETS, 0)
            for i in range(4):
                c = slice(i * D // 4, (i + 1) * D // 4)
                sp.wait_ge(S["h_done"], DEPTH * PER["h_done"] + 2 * (i + 1))
                sp.dma_start(out[0].rearrange("(t p) d -> p t d", p=P)[:, :, c], h[:, :, c]).then_inc(stored, 16)
            sp.wait_ge(stored, 4 * 16)

        @block.gpsimd
        def _(pool):
            got = dict.fromkeys(PER, 0)
            def wait(s, value):
                pool.wait_ge(s, value)
                pool.sem_inc(pool_stood, 1)

            pool.dma_start(pos_i[:], positions[0].partition_broadcast(P)).then_inc(rope_in, 16)
            pool.dma_start(rc[:], rope_c).then_inc(rope_in, 16)
            pool.memset(ident[:], 0.0).then_inc(set_pool, 1)
            pool.memset(within[:], 1.0).then_inc(set_pool, 1)
            pool.memset(ikz[:], 0.0).then_inc(consts, 1)
            pool.memset(eps_c[:], EPS).then_inc(consts, 1)
            pool.memset(one_c[:], 1.0).then_inc(consts, 1)
            for s in acc_free + bank_free:
                pool.sem_inc(s, 1)
            pool.sem_inc(block_done, RAW)
            pool.sem_inc(S["h_done"], NORM)
            pool.wait_ge(set_pool, 2)
            pool.affine_select(out=ident[:], in_=ident[:], compare_op=ALU.not_equal, fill=1.0, base=0,
                               pattern=[[-1, P]], channel_multiplier=1).then_inc(consts, 1)
            pool.memset(within[:].rearrange("p (n c) -> p n c", c=CHUNK)[:, :, 0:1], 0.0).then_inc(consts, 1)

            with pool.Fori(0, DEPTH) as L:
                def at(name, n):
                    return L * PER[name] + n

                def give(name):
                    got[name] += 1
                    return S[name], 1

                def ready(f):
                    b, n = BANK[f]
                    wait(bank_ready[b], L * USES[b] + n + 1)

                def row(src):
                    return src[bass.ds(L, 1)].rearrange("l c -> (l c)").partition_broadcast(P)

                def hide_future(t):
                    v = score[:, t, t * P:(t + 1) * P]
                    return pool.affine_select(out=v, in_=v, compare_op=ALU.is_ge, fill=NEG, base=0,
                                              pattern=[[-1, P]], channel_multiplier=1)

                pool.dma_start(wa2[0:RANK, :], gla_wa2[bass.ds(L, 1)].rearrange("l r c -> (l r) c")) \
                    .then_inc(wa2_in, 16)
                pool.dma_start(gnorm[:], row(gla_norm)).then_inc(gnorm_in, 16)
                for t in range(TT):
                    wait(S["relu_used"], at("relu_used", 4 + 8 * t))
                    hide_future(t).then_inc(*give("causal"))
                for t in range(TT):
                    wait(S["masked"], at("masked", t + 1))
                    hide_future(t).then_inc(*give("allowed"))
                b_at, n_at = BANK["at", 0]
                wait(bank_free[b_at], L * USES[b_at] + n_at + 2)
                for c in range(2):
                    v = at_sb[c * CHUNK:(c + 1) * CHUNK].rearrange("p t g c -> p (t g) c")
                    pool.affine_select(out=v, in_=v, compare_op=ALU.is_ge, fill=0.0, base=0,
                                       pattern=[[0, TT * GH], [1, CHUNK]], channel_multiplier=-1) \
                        .then_inc(*give("at_masked"))
                ready(("pv1", 1))
                pool.dma_start(gpost[:], row(norm_mix_post)).then_inc(gpost_in, 16)
                wait(S["h_done"], at("h_done", NORM + 1))
                pool.dma_start(gpost[:], row(norm_ffn_post)).then_inc(gpost_in, 16)
                wait(S["h_done"], at("h_done", 2 * NORM + 1))
            for n in ("causal", "allowed", "at_masked"):
                assert got[n] == PER[n], (n, got[n])

        @block.scalar
        def _(act):
            got = dict.fromkeys(PER, 0)
            steps = [0]

            def split_hi(number, slot0, landed_n, n=BLK):
                for b in range(QB):
                    act.wait_ge(landed[slot0 + b], landed_n)
                    act.wait_ge(block_done, number + (b + 1 + RAW - HIS))
                    act.activation(hi[:, b, 0:n], raw[:, slot0 + b, 0:n], ACT.Copy).then_inc(hi_done, 1)

            for i, (sin_t, cos_t) in enumerate(((sin_a, cos_a), (sin_i, cos_i))):
                act.wait_ge(set_dve, 2 + 9 * (i + 1))
                act.activation(sin_t, ang[1 + 2 * i][:], ACT.Sin).then_inc(set_act, 1)
                act.activation(cos_t, ang[2 + 2 * i][:], ACT.Sin).then_inc(set_act, 1)
            act.wait_ge(consts, CONSTS)
            act.wait_ge(setup_dma, 16 * SETUP_DMAS)
            act.preload_act_table_set("natural_log_exp_and_others")
            split_hi(0, 0, 16)

            with act.Fori(0, DEPTH) as L:
                n0, l0 = L * (8 * OCTETS), L * (16 * OCTETS)

                def at(name, n):
                    return L * PER[name] + n

                def give(name):
                    got[name] += 1
                    return S[name], 1

                def step(a):
                    steps[0] += 1
                    a.then_inc(act_step, 1)
                    act.wait_ge(act_step, L * ACT_STEPS + steps[0])

                def split(o, half, i8=0, i16=0, n=BLK):
                    split_hi(n0 + i8 + (8 * o + half * QB), half * QB, l0 + i16 + 16 * (o + 1), n)

                def ready(f):
                    b, n = BANK[f]
                    act.wait_ge(bank_ready[b], L * USES[b] + n + 1)
                    return work[:, b, :]

                def taken(f):
                    return bank_free[BANK[f][0]], 1

                def rsqrt(src, cols, scale=1.0, bias=0.0):
                    step(act.activation(stat[:, 2, 0:cols], src, ACT.Ln, scale=scale, bias=bias))
                    act.activation(stat[:, 3, 0:cols], stat[:, 2, 0:cols], ACT.Exp, scale=-0.5) \
                        .then_inc(*give("r0"))

                def pre_norm():
                    for t in range(TT):
                        a = act.activation(facc[:, t, :], h[:, t, :], ACT.Square, accum_out=stat[:, 0, t:t + 1])
                    a.then_inc(*give("ssq"))
                    act.wait_ge(S["ssq"], at("ssq", got["ssq"]))
                    rsqrt(stat[:, 0, 0:TT], TT, 1.0 / D, eps_c[:, 0:1])

                def post_norm(n):
                    act.wait_ge(S["ms"], at("ms", n))
                    rsqrt(stat[:, 1, 0:TT], TT)

                def y_hi(which, g0):
                    for i in range(NORM):
                        bank = ready((f"norm{which}", i))
                        for c in range(2):
                            k = 2 * i + c
                            a = act.activation(y[:, k, 0:SEQ], bank[:, c * SEQ:(c + 1) * SEQ], ACT.Copy,
                                               scale=gains[:, g0 + k:g0 + k + 1])
                        a.then_inc(*give("y_hi"))

                def block_squares(c, src, block):
                    for t in range(TT):
                        a = act.activation(y_scr[:, t, c], src[:, t, :], ACT.Square, accum_out=block(t))
                    return a

                def second_half(pair, number):
                    act.wait_ge(block_done, done(number))
                    act.activation(scr[:, pair], acc[:, 2 * pair:2 * pair + 2, SEQ:2 * SEQ], ACT.Copy) \
                        .then_inc(S["half"], 1)

                def token_out(j, dst):
                    act.wait_ge(block_done, done(n0 + (8 * (O_TOK + j) + RAW - 1)))
                    pair = j % 2
                    for t in range(TT):
                        a = act.activation(dst[:, t, :], acc[:, 2 * pair + t, :], ACT.Copy, scale=pre[:, 0, t:t + 1])
                    a.then_inc(acc_free[pair], 1)

                act.wait_ge(w_gr_in, L * 16 + 16)
                act.activation(gr_hi[:], w_gr[:], ACT.Copy).then_inc(*give("gr_hi"))
                act.wait_ge(S["gains"], at("gains", 1))
                y_hi(1, 0)
                split(0, 1, n=2 * MISC_W)
                split(O_T, 0)
                act.wait_ge(block_done, done(n0 + (RAW - 1)))
                for i, rows in enumerate((MISC_W, RANK)):
                    act.activation(scr[0:rows, 0, i, :], acc[0:rows, 2 * i, SEQ:2 * SEQ], ACT.Copy) \
                        .then_inc(*give("half"))

                def features(g):
                    with act.Fori(0, 2) as i:
                        o = O_T + 2 * g
                        for half in range(2):
                            split(o + half, 1 - half, i * 8, i * 16)
                            second_half(half, n0 + i * 8 + (8 * o + half * QB + QB - 1))

                act.wait_ge(S["h_done"], at("h_done", NORM))
                pre_norm()
                for i in range(2):
                    act.wait_ge(acc_free[i], L * PAIR_USES + (A_MISC + 2))
                features(0)
                features(1)
                features(2)
                for i in range(2):
                    bank = ready(("z", i))
                    for c in range(2):
                        g = 2 * i + c
                        a = act.activation(za[:, g, :], bank[:, c * SEQ:(c + 1) * SEQ], ACT.Identity,
                                           bias=gains[:, 2 * KT + g:2 * KT + g + 1])
                    a.then_inc(*taken(("z", i)))
                features(3)
                act.wait_ge(S["zabs"], at("zabs", 1))
                step(act.activation(zb[:], zb[:], ACT.Exp, scale=-1.0))
                act.activation(zb[:], zb[:], ACT.Ln, bias=one_c[:, 0:1]).then_inc(*give("zl"))
                for n, f in enumerate([("log0", i) for i in range(4)] + [("log1", i) for i in range(8)]):
                    bank = ready(f)
                    if n >= BANKS:
                        act.wait_ge(S["relu_used"], at("relu_used", n - BANKS + 1))
                    act.activation(relus[:, n % BANKS, :], bank, ACT.Relu).then_inc(*taken(f))

                def exps(t):
                    act.wait_ge(S["negmax"], at("negmax", t + 1))
                    for a in range(AH):
                        v = probs[:, a, 0:(t + 1) * P]
                        e = act.activation(v, v, ACT.Exp, bias=smax[:, 0, a:a + 1], accum_out=smax[:, 1, a:a + 1])
                    e.then_inc(*give("expd"))

                def transposed_probs(t):
                    for i in range((t + 1) * 2):
                        f = (f"pt{t}", i)
                        if t == 0:
                            dst = ptT[:, 4 * i:4 * i + 4, 0, :]
                        else:
                            dst = ptT[:, 2 * i:2 * i + 2, :, :].rearrange("p a j q -> p (a j) q")
                        act.activation(dst, ready(f).rearrange("p (a q) -> p a q", q=P), ACT.Copy) \
                            .then_inc(*taken(f))

                def attended(t):
                    for i in range(2):
                        k0 = KT // 2 + 4 * i
                        act.activation(oT[:, k0:k0 + 4, t * P:(t + 1) * P],
                                       ready((f"pv{t}", i)).rearrange("p (a q) -> p a q", q=P), ACT.Copy) \
                            .then_inc(*give("pv_hi"))

                def gate_exp(j):
                    act.wait_ge(acc_free[j], L * PAIR_USES + (A_TOK + 2 + 2))
                    act.activation(scr_gate[:, :, j, :], gg[:, :, 512 * j:512 * j + 512], ACT.Exp, scale=-1.0) \
                        .then_inc(*give("gate_e"))

                split(O_TOK, 1)
                split(O_TOK + 1, 0)
                act.wait_ge(S["rstd"], at("rstd", 1))
                token_out(0, dv[:, :, 0:512])
                split(O_TOK + 1, 1)
                split(O_TOK + 2, 0)
                token_out(1, dv[:, :, 512:1024])
                exps(0)
                split(O_TOK + 2, 1)
                act.wait_ge(S["zsc"], at("zsc", 1))
                act.activation(za[:], zb[:], ACT.Exp, scale=1.0 / TAU).then_inc(*give("eb"))
                act.activation(kinv[:], zb[:], ACT.Exp, scale=-1.0 / TAU).then_inc(*give("enb"))
                split(O_TOK + 3, 0)
                token_out(2, gv[:, :, 0:512])
                transposed_probs(0)
                split(O_TOK + 3, 1)
                exps(1)
                act.wait_ge(S["edin"], at("edin", 1))
                act.activation(za[:], za[:], ACT.Exp, scale=-1.0 / TAU).then_inc(*give("edec"))
                split(O_TOK + 4, 0)
                token_out(3, gv[:, :, 512:1024])
                attended(0)
                transposed_probs(1)
                for t in range(TT):
                    act.activation(kd[:, t, :], ready(("kd", t)), ACT.Copy).then_inc(*taken(("kd", t)))
                act.activation(at_sb[:].rearrange("p t g c -> p (t g c)"), ready(("at", 0)), ACT.Copy) \
                    .then_inc(*taken(("at", 0)))
                split(O_TOK + 4, 1)
                split(O_TOK + 5, 0)
                token_out(4, gg[:, :, 0:512])
                attended(1)
                gate_exp(0)
                split(O_TOK + 5, 1)
                split(O_OUT, 0)
                token_out(5, gg[:, :, 512:1024])
                gate_exp(1)
                for t in range(TT):
                    for gp in range(2):
                        bank = ready(("o", 2 * t + gp))
                        for c in range(2):
                            g = t * GH + 2 * gp + c
                            a = act.activation(y_scr[:, 0, g * DV:(g + 1) * DV], bank[:, c * DV:(c + 1) * DV], ACT.Square,
                                               accum_out=stat[:, 0, g:g + 1])
                        a.then_inc(*give("ossq"))
                act.wait_ge(S["ossq"], at("ossq", PER["ossq"]))
                rsqrt(stat[:, 0, 0:TT * GH], TT * GH, 1.0 / DV, eps_c[:, 0:1])
                split(O_OUT, 1)
                for i in range(4):
                    act.activation(oT[:, 2 * i:2 * i + 2, 0:SEQ],
                                   ready(("ot", i)).rearrange("p (k q) -> p k q", q=SEQ), ACT.Copy) \
                        .then_inc(*give("ot_hi"))

                for j in range(4):
                    if j:
                        split(O_OUT + j, 1)
                    split(O_OUT + j + 1, 0)
                    act.wait_ge(block_done, done(n0 + (8 * (O_OUT + j) + RAW - 1)))
                    block_squares(slice(512 * j, 512 * (j + 1)), acc[:, 2 * (j % 2):2 * (j % 2) + 2, :],
                                  lambda t: stat[:, 0, 4 * t + j:4 * t + j + 1]).then_inc(*give("ssq"))

                post_norm(1)
                y_hi(2, KT)

                def quarter(q, first=False, last=False):
                    with act.Fori(0, UP) as i:
                        i8 = (i + q * (UP + DN)) * 8
                        for half in range(2):
                            split(O_FFN + half, 1 - half, i8, i8 * 2)
                            second_half(half, n0 + i8 + (8 * O_FFN + half * QB + QB - 1))
                            act.wait_ge(S["squared"], i * 2 + q * 8 + at("squared", 1 + half))
                            act.activation(u[:, bass.ds(i * 4 + 2 * half, 2), 0:SEQ], u2[:, half], ACT.Copy) \
                                .then_inc(S["u_hi"], 1)
                    if first:
                        act.wait_ge(S["h_done"], at("h_done", 2 * NORM))
                        pre_norm()
                    with act.Fori(0, DN // 2) as i:
                        i8 = (i * 2 + q * (UP + DN)) * 8
                        for j in range(2):
                            split(O_FFN + UP + j, 1, i8, i8 * 2)
                            split(O_FFN + UP + j + 1, 0, i8, i8 * 2)
                            if last:
                                act.wait_ge(acc_free[j], i + (L * PAIR_USES + (PAIR_USES - DN // 2 + 2)))
                                c = bass.ds(i * 1024 + j * 512, 512)
                                block_squares(c, facc[:, :, c],
                                              lambda t: stat[:, 0, bass.ds(i * 2 + (4 * t + j), 1)]) \
                                    .then_inc(S["ssq"], 1)

                quarter(0, first=True)
                with act.Fori(1, NQ - 1) as q:
                    quarter(q)
                quarter(NQ - 1, last=True)

                post_norm(2)
                act.wait_ge(S["h_done"], at("h_done", 2 * NORM + 1))
            assert steps[0] == ACT_STEPS, steps
            for n in ("gr_hi", "y_hi", "r0", "zl", "eb", "enb", "edec", "expd", "pv_hi", "ossq",
                      "ot_hi", "gate_e"):
                assert got[n] == PER[n], (n, got[n])

        @block.tensor
        def _(pe):
            pe.wait_ge(consts, CONSTS)
            pe.wait_ge(setup_dma, 16 * SETUP_DMAS)
            pe.transpose(work[:, 0, 0:DEPTH * NG], gains_in[0:DEPTH * NG, :], ident[0:DEPTH * NG, 0:DEPTH * NG]) \
                .then_inc(set_pe, 1)
            pe.wait_ge(set_dve, 1)

            with pe.Fori(0, DEPTH) as L:
                n0, p0 = L * (8 * OCTETS), L * PAIR_USES

                def at(name, n):
                    return L * PER[name] + n

                def need(name, n=None):
                    pe.wait_ge(S[name], at(name, PER[name] if n is None else n))

                def fill(f):
                    b, n = BANK[f]
                    pe.wait_ge(bank_free[b], L * USES[b] + n + 1)
                    return work[:, b, :]

                def filled(f):
                    return bank_ready[BANK[f][0]], 1

                def taken(f):
                    b, n = BANK[f]
                    pe.wait_ge(bank_free[b], L * USES[b] + n + 2)

                def norm_transposes(which, chunks):
                    for i in chunks:
                        bank = fill((f"norm{which}", i))
                        pe.wait_ge(S["h_done"], at("h_done", (which - 1) * NORM + i + 1))
                        for c in range(2):
                            for t in range(TT):
                                k = 2 * i + c
                                mm = pe.transpose(bank[:, c * SEQ + t * P:c * SEQ + (t + 1) * P],
                                                  h[:, t, k * P:(k + 1) * P], ident[:])
                        mm.then_inc(*filled((f"norm{which}", i)))

                def feature_products(bank, w_lo, w_hi, k):
                    last = k == KT - 1
                    if k == 0:
                        pe.matmul(bank, w_hi, y[:, k, :], start=True, stop=False)
                        return pe.matmul(bank[:, 0:SEQ], w_lo, y[:, k, 0:SEQ], start=False, stop=False)
                    pe.matmul(bank[:, 0:SEQ], w_lo, y[:, k, 0:SEQ], start=False, stop=False)
                    return pe.matmul(bank, w_hi, y[:, k, :], start=False, stop=last)

                def feature_octet(number, uses, before=None):
                    for half in range(2):
                        pe.wait_ge(acc_free[half], uses + 1)
                        for b in range(QB):
                            j = half * QB + b
                            if before and half == 0:
                                before(b)
                            pe.wait_ge(lo_done, number + (j + 1))
                            lo_b = lo[:, j, :].rearrange("p (k c) -> p k c", k=4)
                            hi_b = hi[:, b, :].rearrange("p (k c) -> p k c", k=4)
                            for kk in range(4):
                                for c in range(2):
                                    mm = feature_products(acc[:, 2 * half + c, :], lo_b[:, kk, c * P:(c + 1) * P],
                                                          hi_b[:, kk, c * P:(c + 1) * P], 4 * b + kk)
                            mm.then_inc(block_done, 1)

                def token_octet(number, pair, uses, xs, order, before=None):
                    pe.wait_ge(acc_free[pair], uses + 1)
                    for j in range(RAW):
                        if before:
                            before(j)
                        pe.wait_ge(lo_done, number + (j + 1))
                        lo_b = lo[:, j, :].rearrange("p (k c) -> p k c", k=2)
                        hi_b = hi[:, j % HIS, :].rearrange("p (k c) -> p k c", k=2)
                        for kk in range(2):
                            k = order[j] + kk
                            first, last = j == 0 and kk == 0, j == RAW - 1 and kk == 1
                            for t in range(TT):
                                x_hi, x_lo = xs[:, k, t * P:(t + 1) * P], xs[:, k, SEQ + t * P:SEQ + (t + 1) * P]
                                a = acc[:, 2 * pair + t, :]
                                pe.matmul(a, x_hi, lo_b[:, kk, :], start=first, stop=False)
                                pe.matmul(a, x_hi, hi_b[:, kk, :], start=False, stop=False)
                                mm = pe.matmul(a, x_lo, hi_b[:, kk, :], start=False, stop=last)
                        mm.then_inc(block_done, 1)

                for j in range(RAW):
                    norm_transposes(1, range(BANKS) if j == 0 else [j + BANKS - 1] if j + BANKS - 1 < NORM else [])
                    if j == 0:
                        need("gr_lo")
                        for i in range(2):
                            pe.wait_ge(acc_free[i], p0 + (A_MISC + 1))
                    taken(("norm1", j))
                    pe.wait_ge(lo_done, n0 + (j + 1))
                    w = 512 if j < QB else MISC_W
                    lo_b = lo[:, j, 0:2 * w].rearrange("p (k c) -> p k c", k=2)[:, :, w - MISC_W:w]
                    hi_b = hi[:, j % HIS, 0:2 * w].rearrange("p (k c) -> p k c", k=2)[:, :, w - MISC_W:w]
                    for kk in range(2):
                        k = 2 * j + kk
                        feature_products(acc[0:RANK, 2, :], gr_lo[:, k, :], gr_hi[:, k, :], k)
                        mm = feature_products(acc[0:MISC_W, 0, :], lo_b[:, kk, :], hi_b[:, kk, :], k)
                    mm.then_inc(block_done, 1)

                def features(g):
                    with pe.Fori(0, 2) as i:
                        feature_octet(n0 + i * 8 + 8 * (O_T + 2 * g), p0 + i + (A_T + 2 * g))

                features(0)
                features(1)
                rb_bank = fill(("rb", 0))
                need("rstd", 1)
                for t in range(TT):
                    mm = pe.transpose(rb_bank[:, t * P:(t + 1) * P], pre[:, 0, t:t + 1].to_broadcast([P, P]), ident[:])
                mm.then_inc(*filled(("rb", 0)))
                features(2)
                need("scaled")
                pe.wait_ge(wa2_in, L * 16 + 16)
                iw_bank = fill(("iw", 0))
                for i in range(2):
                    bank = fill(("z", i))
                    for c in range(2):
                        g = 2 * i + c
                        mm = pe.matmul(bank[:, c * SEQ:(c + 1) * SEQ], wa2[0:RANK, g * DK:(g + 1) * DK],
                                       gr[0:RANK, :], start=True, stop=True)
                    mm.then_inc(*filled(("z", i)))
                for t in range(TT):
                    mm = pe.transpose(iw_bank[:, t * IH:(t + 1) * IH], misc[DI:DI + IH, t * P:(t + 1) * P],
                                      ident[DI:DI + IH, DI:DI + IH])
                mm.then_inc(*filled(("iw", 0)))
                features(3)
                need("rot", 36)
                for i in range(4):
                    bank = fill(("log0", i))
                    for c in range(2):
                        mm = pe.matmul(bank[:, c * SEQ:(c + 1) * SEQ], ts[:, T_IQ + 2 * i + c, 0:P],
                                       ikz[:, :, 0:P], start=True, stop=True)
                    mm.then_inc(*filled(("log0", i)))
                for i in range(8):
                    bank = fill(("log1", i))
                    pe.matmul(bank, ts[:, T_IQ + i, P:SEQ], ikz[:], start=True, stop=True) \
                        .then_inc(*filled(("log1", i)))

                def scores(t):
                    keys = (t + 1) * P
                    heads = 512 // keys
                    if t == 0:
                        need("rot")
                    for i in range(AH // heads):
                        bank = fill((f"sc{t}", i))
                        for c in range(heads):
                            a = heads * i + c
                            mm = pe.matmul(bank[:, c * keys:(c + 1) * keys], ts[:, T_DQ + a, t * P:(t + 1) * P],
                                           ts[:, T_DK + a, 0:keys], start=True, stop=True)
                        mm.then_inc(*filled((f"sc{t}", i)))

                def transpose_probs(t):
                    need("probs", t + 1)
                    for i in range(2 * (t + 1)):
                        bank = fill((f"pt{t}", i))
                        for c in range(4):
                            a, j = (4 * i + c, 0) if t == 0 else (2 * i + c // 2, c % 2)
                            mm = pe.transpose(bank[:, c * P:(c + 1) * P], probs[:, a, j * P:(j + 1) * P], ident[:])
                        mm.then_inc(*filled((f"pt{t}", i)))

                def attend(t):
                    taken((f"pt{t}", 2 * t + 1))
                    for i in range(2):
                        bank = fill((f"pv{t}", i))
                        for c in range(4):
                            a = 4 * i + c
                            for j in range(t + 1):
                                mm = pe.matmul(bank[:, c * P:(c + 1) * P], dv[:, j, a * DH:(a + 1) * DH],
                                               ptT[:, a, j, :], start=(j == 0), stop=(j == t))
                        mm.then_inc(*filled((f"pv{t}", i)))

                straight = [2 * b for b in range(RAW)]

                def tok(j):
                    token_octet(n0 + 8 * (O_TOK + j), j % 2, p0 + (A_TOK + j // 2), y, straight)

                tok(0)
                tok(1)
                scores(0)
                tok(2)
                transpose_probs(0)
                scores(1)
                tok(3)
                for j in range(2):
                    pe.wait_ge(acc_free[j], p0 + (A_TOK + 2))
                for i in range(2):
                    taken(("pt0", i))
                attend(0)
                transpose_probs(1)
                need("gla_q")
                need("gla_kinv")
                need("gla_k")
                at_bank = fill(("at", 0))
                for t in range(TT):
                    bank = fill(("kd", t))
                    for g in range(GH):
                        mm = pe.transpose(bank[:, g * DK:(g + 1) * DK], ts[:, T_GK + g, t * P:(t + 1) * P], ident[:])
                    mm.then_inc(*filled(("kd", t)))
                for n in range(NCH):
                    t, c = n // 2, n % 2
                    for g in range(GH):
                        col = (t * GH + g) * CHUNK
                        mm = pe.matmul(at_bank[c * CHUNK:(c + 1) * CHUNK, col:col + CHUNK],
                                       kinv[:, g, n * CHUNK:(n + 1) * CHUNK],
                                       ts[:, T_GQ + g, n * CHUNK:(n + 1) * CHUNK], start=True, stop=True)
                mm.then_inc(*filled(("at", 0)))
                tok(4)
                for i in range(4):
                    taken(("pt1", i))
                attend(1)
                for j in range(2):
                    pe.wait_ge(acc_free[j], p0 + (A_TOK + 3))
                for t in range(TT):
                    taken(("kd", t))
                for n in range(NCH - 1):
                    t, rows = n // 2, slice((n % 2) * CHUNK, (n % 2 + 1) * CHUNK)
                    for gp in range(2):
                        bank = fill(("ds", 2 * n + gp))
                        for c in range(2):
                            g = 2 * gp + c
                            mm = pe.matmul(bank[:, c * DV:(c + 1) * DV], kd[rows, t, g * DK:(g + 1) * DK],
                                           gv[rows, t, g * DV:(g + 1) * DV], start=True, stop=True)
                        mm.then_inc(*filled(("ds", 2 * n + gp)))
                tok(5)
                taken(("at", 0))
                need("at_masked")
                for i in range(6):
                    taken(("ds", i))
                for t in range(TT):
                    for gp in range(2):
                        bank = fill(("o", 2 * t + gp))
                        pe.sem_inc(pe_stood, 1)
                        for c in range(2):
                            g = 2 * gp + c
                            for half in range(2):
                                n = 2 * t + half
                                rows = slice(half * CHUNK, (half + 1) * CHUNK)
                                o = bank[rows, c * DV:(c + 1) * DV]
                                mm = pe.matmul(o, at_sb[rows, t, g, :], gv[rows, t, g * DV:(g + 1) * DV],
                                               start=True, stop=(n == 0))
                                if n:
                                    mm = pe.matmul(o, ts[:, T_GQ + g, n * CHUNK:(n + 1) * CHUNK],
                                                   states[:, n - 1, g, :], start=False, stop=True)
                        mm.then_inc(*filled(("o", 2 * t + gp)))
                def o_in_place(j):
                    if j == 0:
                        for i in range(2):
                            taken(("pv1", i))
                    if j == RAW // 2:
                        for i in range(4):
                            taken(("o", i))
                        for i in range(4):
                            bank = fill(("ot", i))
                            for c in range(2):
                                for t in range(TT):
                                    k = 2 * i + c
                                    mm = pe.transpose(bank[:, c * SEQ + t * P:c * SEQ + (t + 1) * P],
                                                      gg[:, t, k * P:(k + 1) * P], ident[:])
                            mm.then_inc(*filled(("ot", i)))
                    if j >= RAW // 2:
                        taken(("ot", j - RAW // 2))

                for j in range(4):
                    token_octet(n0 + 8 * (O_OUT + j), j % 2, p0 + (A_OUT + j // 2), oT, OUT_ROWS,
                                None if j else o_in_place)

                def y_in_place(b):
                    norm_transposes(2, range(4) if b == 0 else range(2 * b + 2, 2 * b + 4) if b < 3 else [])
                    taken(("norm2", 2 * b))
                    taken(("norm2", 2 * b + 1))

                def up_octet(q, i, before=None):
                    feature_octet(i * 8 + q * (8 * (UP + DN)) + (n0 + 8 * O_FFN), i + q * (UP + DN // 2) + (p0 + A_FFN),
                                  before)

                def quarter(q, first=0):
                    with pe.Fori(first, UP) as i:
                        up_octet(q, i)

                    def u_in_place(j):
                        pe.wait_ge(S["u_lo"], q * 8 + at("u_lo", j + 1))

                    with pe.Fori(0, DN // 2) as i:
                        for j in range(2):
                            token_octet(i * 16 + q * (8 * (UP + DN)) + (n0 + 8 * (O_FFN + UP + j)), j,
                                        i + q * (UP + DN // 2) + (p0 + (A_FFN + UP)), u, straight, u_in_place)

                up_octet(0, 0, y_in_place)
                quarter(0, 1)
                with pe.Fori(1, NQ) as q:
                    quarter(q)

        @block.vector
        def _(dve):
            got = dict.fromkeys(PER, 0)
            steps = [0]
            two_pi = 2 * np.pi
            c1 = 6.28125
            c2 = float(np.uint32(np.float32(two_pi - c1).view(np.uint32) & np.uint32(0xFFFFF000)).view(np.float32))
            c3 = float(np.float32(two_pi - c1 - c2))
            magic = float(1.5 * 2 ** 23)
            below_pi = 3.1415925

            def split_lo(number, slot0, n=BLK):
                for b in range(QB):
                    dve.wait_ge(hi_done, number + (b + 1))
                    dve.tensor_tensor(lo[:, slot0 + b, 0:n], raw[:, slot0 + b, 0:n],
                                      hi[:, b, 0:n].bitcast(F32), ALU.subtract).then_inc(lo_done, 1)

            n_set = [0]

            def set_up(i):
                n_set[0] += 1
                i.then_inc(set_dve, 1)
                dve.wait_ge(set_dve, n_set[0])

            dve.wait_ge(set_pe, 1)
            set_up(dve.tensor_copy(gains_all[:].rearrange("p l n -> p (l n)"), work[:, 0, 0:DEPTH * NG]))
            dve.wait_ge(rope_in, 32)
            set_up(dve.tensor_copy(ang[0][:], pos_i[:]))
            for i in range(2):
                a, turns, c = ang[1 + 2 * i][:], ang[5][:], ang[2 + 2 * i][:]
                set_up(dve.tensor_scalar(a, ang[0][:], rc[:, 2 * i:2 * i + 1], None, ALU.mult))
                set_up(dve.tensor_scalar(turns, a, 1 / two_pi, magic, ALU.mult, ALU.add))
                set_up(dve.tensor_scalar(turns, turns, magic, None, ALU.subtract))
                for part in (c1, c2, c3):
                    set_up(dve.scalar_tensor_tensor(a, turns, -part, a, ALU.mult, ALU.add))
                set_up(dve.tensor_scalar(a, a, below_pi, -below_pi, ALU.min, ALU.max))
                set_up(dve.scalar_tensor_tensor(c, a, -1.0, a, ALU.mult, ALU.max))
                set_up(dve.tensor_scalar(c, c, -1.0, np.pi / 2, ALU.mult, ALU.add))
            dve.wait_ge(set_act, 4)
            for i, s in enumerate((sin_a, sin_i)):
                set_up(dve.tensor_scalar(s, s, rc[:, 2 * i + 1:2 * i + 2], None, ALU.mult))
            dve.wait_ge(consts, CONSTS)
            dve.wait_ge(setup_dma, 16 * SETUP_DMAS)
            split_lo(0, 0)

            with dve.Fori(0, DEPTH) as L:
                n0 = L * (8 * OCTETS)

                def at(name, n):
                    return L * PER[name] + n

                def need(name, n=None):
                    dve.wait_ge(S[name], at(name, PER[name] if n is None else n))

                def give(name):
                    got[name] += 1
                    return S[name], 1

                def step(i):
                    steps[0] += 1
                    i.then_inc(dve_step, 1)
                    dve.wait_ge(dve_step, L * DVE_STEPS + steps[0])

                def held():
                    dve.sem_inc(dve_stood, 1)

                def split(o, half, i8=0, n=BLK):
                    split_lo(n0 + i8 + (8 * o + half * QB), half * QB, n)

                def ready(f):
                    b, n = BANK[f]
                    dve.wait_ge(bank_ready[b], L * USES[b] + n + 1)
                    return work[:, b, :]

                def in_sbuf(f):
                    b, n = BANK[f]
                    dve.wait_ge(bank_free[b], L * USES[b] + n + 2)

                def taken(f):
                    return bank_free[BANK[f][0]], 1

                def newton(cols):
                    ms, r0, a, r = (stat[:, i, 0:cols] for i in (1, 3, 4, 5))
                    got["r0"] += 1
                    dve.wait_ge(S["r0"], at("r0", got["r0"]))
                    step(dve.tensor_tensor(a, ms, r0, ALU.mult))
                    step(dve.tensor_tensor(a, a, r0, ALU.mult))
                    step(dve.tensor_scalar(a, a, -0.5, 1.5, ALU.mult, ALU.add))
                    step(dve.tensor_tensor(r, r0, a, ALU.mult))

                def rstd_of(size, cols):
                    step(dve.tensor_scalar(stat[:, 1, 0:cols], stat[:, 0, 0:cols], 1.0 / size, EPS, ALU.mult, ALU.add))
                    newton(cols)

                def pre_norm(n):
                    dve.wait_ge(S["ssq"], at("ssq", n))
                    rstd_of(D, TT)
                    r = stat[:, 5, 0:TT]
                    dve.tensor_copy(pre[:, 0, :], r)
                    dve.tensor_tensor(pre[:, 1, :], r, r, ALU.mult)
                    dve.tensor_scalar(pre[:, 2, :], r, float(DH ** -0.5), None, ALU.mult).then_inc(*give("rstd"))
                    dve.wait_ge(S["rstd"], at("rstd", got["rstd"]))
                    held()

                def update(i, which):
                    c = slice(i * D // NORM, (i + 1) * D // NORM)
                    for t in range(TT):
                        v = dve.scalar_tensor_tensor(h[:, t, c], facc[:, t, c], stat[:, 5, t:t + 1], h[:, t, c],
                                                     ALU.mult, ALU.add)
                    v.then_inc(*give("h_done"))

                def y_lo(i, which, g0):
                    f = (f"norm{which}", i)
                    dve.wait_ge(S["y_hi"], at("y_hi", 8 * (which - 1) + i + 1))
                    for c in range(2):
                        k = 2 * i + c
                        v = dve.scalar_tensor_tensor(
                            y[:, k, SEQ:2 * SEQ], work[:, BANK[f][0], c * SEQ:(c + 1) * SEQ],
                            gains[:, g0 + k:g0 + k + 1], y[:, k, 0:SEQ].bitcast(F32), ALU.mult, ALU.subtract)
                    v.then_inc(*taken(f))

                def mean_squares():
                    step(dve.tensor_reduce(stat[:, 4, 0:TT], stat[:, 0, :].rearrange("p (t b) -> p t b", t=TT),
                                           AX_X, ALU.add))
                    dve.tensor_scalar(stat[:, 1, 0:TT], stat[:, 4, 0:TT], 1.0 / D, EPS, ALU.mult, ALU.add) \
                        .then_inc(*give("ms"))

                def weigh(dst, src):
                    return dve.tensor_tensor(dst, src[0], src[1].unsqueeze(1).to_broadcast([P, TT, 512]), ALU.mult)

                def rope(v, cos, sin, mask, count, dst):
                    sw = swapped[0:v.shape[0], 0:v.shape[1], :] if len(v.shape) == 3 else swapped[0:v.shape[0], 0, :]
                    if len(v.shape) == 3:
                        cos, sin = (x.unsqueeze(1).to_broadcast(list(v.shape)) for x in (cos, sin))
                    held()
                    dve.stream_shuffle(sw, v, mask).then_inc(S["rot"], 1)
                    dve.wait_ge(S["rot"], count(1))
                    dve.tensor_tensor(sw, sw, sin, ALU.mult).then_inc(S["rot"], 1)
                    dve.tensor_tensor(v, v, cos, ALU.mult).then_inc(S["rot"], 1)
                    dve.wait_ge(S["rot"], count(3))
                    for d in dst[:-1]:
                        dve.tensor_tensor(d, v, sw, ALU.add)
                    dve.tensor_tensor(dst[-1], v, sw, ALU.add).then_inc(S["rot"], 1)
                    dve.wait_ge(S["rot"], count(4))

                dve.tensor_copy(gains[:], gains_all[:, bass.ds(L, 1), :].rearrange("p l n -> p (l n)")) \
                    .then_inc(*give("gains"))
                dve.wait_ge(S["gains"], at("gains", 1))
                need("gr_hi")
                dve.tensor_tensor(gr_lo[:], w_gr[:], gr_hi[:].bitcast(F32), ALU.subtract).then_inc(*give("gr_lo"))
                for i in range(NORM):
                    y_lo(i, 1, 0)
                split(0, 1, n=2 * MISC_W)
                split(O_T, 0)
                for i, (rows, dst) in enumerate(((MISC_W, misc), (RANK, gr))):
                    dve.wait_ge(S["half"], at("half", i + 1))
                    dve.tensor_tensor(dst[0:rows, :], acc[0:rows, 2 * i, 0:SEQ], scr[0:rows, 0, i, :], ALU.add) \
                        .then_inc(acc_free[i], 1)

                def features(g):
                    with dve.Fori(0, 2) as i:
                        for half in range(2):
                            split(O_T + 2 * g + half, 1 - half, i * 8)
                            dve.wait_ge(S["half"], i * 2 + at("half", 3 + 4 * g + half))
                            v, dst = fresh[:, half], ts[:, bass.ds(i * 4 + (8 * g + 2 * half), 2), :]
                            dve.tensor_tensor(v, acc[:, 2 * half:2 * half + 2, 0:SEQ], scr[:, half], ALU.add) \
                                .then_inc(acc_free[half], 1)
                            dve.wait_ge(acc_free[half], i + (L * PAIR_USES + (A_T + 2 * g + 2)))
                            count = lambda n: i * 8 + at("rot", 16 * g + (4 if g == 2 else 0) + 4 * half + n)
                            if g == 0:
                                rope(v, cos_i, sin_i, swap_mask(8), count, [dst])
                            elif g == 1:
                                rope(v, cos_a, sin_a, swap_mask(16), count, [dst])
                            elif g == 2:
                                rope(v, rot_k[:, 0, :], rot_k[:, 1, :], swap_mask(16), count, [dst])
                            else:
                                dve.tensor_tensor(dst, v, rb[:].unsqueeze(1).to_broadcast([P, 2, SEQ]), ALU.mult)

                features(0)
                pre_norm(S_PRE)
                features(1)
                dve.tensor_copy(rb[:], ready(("rb", 0))[:, 0:SEQ]).then_inc(*taken(("rb", 0)))
                in_sbuf(("rb", 0))
                step(dve.tensor_tensor(rot_k[:], rot_a[:], rb[:].unsqueeze(1).to_broadcast([P, 2, SEQ]), ALU.mult))
                dve.tensor_tensor(misc[0:MISC_W, :], misc[0:MISC_W, :], rb[0:MISC_W, :], ALU.mult)
                dve.tensor_tensor(gr[0:RANK, :], gr[0:RANK, :], rb[0:RANK, :], ALU.mult).then_inc(*give("scaled"))
                need("scaled")
                rope(misc[0:DI, :], cos_i[0:DI, :], sin_i[0:DI, :], swap_mask(8),
                     lambda n: at("rot", 32 + n), [ikz[0:DI, 0, :], ikz[DI:2 * DI, 1, :]])
                held()
                features(2)
                bank = ready(("iw", 0))
                for t in range(TT):
                    v = dve.tensor_scalar(iw[:, t, :], bank[:, t * IH:(t + 1) * IH], pre[:, 0, t:t + 1],
                                          float(IH ** -0.5 * DI ** -0.5), ALU.mult, ALU.mult)
                v.then_inc(*taken(("iw", 0)))
                in_sbuf(("z", 0))
                in_sbuf(("z", 1))
                dve.scalar_tensor_tensor(zb[:], za[:], -1.0, za[:], ALU.mult, ALU.max).then_inc(*give("zabs"))
                features(3)

                def sum_heads(t, i, n):
                    keys = (t + 1) * P
                    heads = 512 // keys
                    in_sbuf((f"log{t}", i))
                    for c in range(heads):
                        head = heads * i + c
                        r = relus[:, n % BANKS, c * keys:(c + 1) * keys]
                        s = score[:, t, 0:keys]
                        w = iw[:, t, head:head + 1]
                        if head == 0:
                            v = dve.tensor_scalar(s, r, w, None, ALU.mult)
                        else:
                            v = dve.scalar_tensor_tensor(s, r, w, s, ALU.mult, ALU.add)
                        if c < heads - 1:
                            step(v)
                    v.then_inc(*give("relu_used"))
                    dve.wait_ge(S["relu_used"], at("relu_used", n + 1))

                def top_k(t):
                    s = score[:, t, 0:(t + 1) * P]
                    need("causal", t + 1)
                    for _ in range(TOPK // 8):
                        held()
                        step(dve.max(top8[:], s))
                        held()
                        step(dve.match_replace(s, top8[:], s, TAKEN))
                    dve.tensor_scalar(s, s, 10 * NEG, NEG, ALU.is_gt, ALU.mult).then_inc(*give("masked"))

                for t in range(TT):
                    for i in range(4 * (t + 1)):
                        sum_heads(t, i, 4 * t + i)

                def softmax_in(t):
                    keys = (t + 1) * P
                    heads = 512 // keys
                    need("allowed", t + 1)
                    bias = score[:, t, 0:keys].unsqueeze(1).to_broadcast([P, heads, keys])
                    for i in range(AH // heads):
                        f = (f"sc{t}", i)
                        bank = ready(f).rearrange("p (a q) -> p a q", q=keys)
                        dve.scalar_tensor_tensor(probs[:, heads * i:heads * (i + 1), 0:keys], bank, pre[:, 2, t:t + 1],
                                                 bias, ALU.mult, ALU.add).then_inc(*taken(f))
                        in_sbuf(f)
                    step(dve.tensor_reduce(smax[:, 0, :], probs[:, :, 0:keys], AX_X, ALU.max))
                    dve.tensor_scalar(smax[:, 0, :], smax[:, 0, :], -1.0, None, ALU.mult).then_inc(*give("negmax"))

                def softmax_out(t):
                    keys = (t + 1) * P
                    need("expd", t + 1)
                    step(dve.reciprocal(smax[:, 2, :], smax[:, 1, :]))
                    v = probs[:, :, 0:keys]
                    dve.tensor_tensor(v, v, smax[:, 2, :].unsqueeze(2).to_broadcast([P, AH, keys]), ALU.mult) \
                        .then_inc(*give("probs"))

                def attended_lo(t):
                    for i in range(2):
                        f, k0 = (f"pv{t}", i), KT // 2 + 4 * i
                        need("pv_hi", 2 * t + i + 1)
                        dve.tensor_tensor(oT[:, k0:k0 + 4, SEQ + t * P:SEQ + (t + 1) * P],
                                          work[:, BANK[f][0], :].rearrange("p (a q) -> p a q", q=P),
                                          oT[:, k0:k0 + 4, t * P:(t + 1) * P].bitcast(F32), ALU.subtract) \
                            .then_inc(*taken(f))

                def gate(j):
                    need("gate_e", j + 1)
                    e, g = scr_gate[:, :, j, :], gg[:, :, 512 * j:512 * j + 512]
                    step(dve.tensor_scalar(e, e, 1.0, None, ALU.add))
                    step(dve.reciprocal(e, e))
                    step(dve.tensor_tensor(g, g, e, ALU.mult))
                    if j == 0:
                        dve.wait_ge(gnorm_in, L * 16 + 16)
                    for t in range(TT):
                        v = g[:, t, :].rearrange("p (g c) -> p g c", c=DV)
                        step(dve.tensor_tensor(v, v, gnorm[:].unsqueeze(1).to_broadcast([P, 2, DV]), ALU.mult))

                split(O_TOK, 1)
                top_k(0)
                split(O_TOK + 1, 0)
                top_k(1)
                split(O_TOK + 1, 1)
                split(O_TOK + 2, 0)
                softmax_in(0)
                need("zl")
                step(dve.scalar_tensor_tensor(za[:], za[:], 0.0, zb[:], ALU.min, ALU.subtract))
                for g in range(GH):
                    v = dve.tensor_tensor_scan(zb[:, g, :], within[:], za[:, g, :], 0.0, ALU.mult, ALU.add)
                v.then_inc(*give("zsc"))
                need("zsc")
                split(O_TOK + 2, 1)
                softmax_out(0)
                split(O_TOK + 3, 0)
                need("eb")
                v = ts[:, T_GQ:T_GQ + GH, :]
                dve.scalar_tensor_tensor(v, v, float(DK ** -0.5), za[:], ALU.mult, ALU.mult).then_inc(*give("gla_q"))
                zc = za[:].rearrange("p g (n c) -> p (g n) c", c=CHUNK)
                step(dve.tensor_copy(decay[:].rearrange("p g n -> p (g n)"), zc[:, :, CHUNK - 1]))
                need("gla_q")
                bc = zb[:].rearrange("p g (n c) -> p (g n) c", c=CHUNK)
                dve.tensor_tensor(zc, bc, bc[:, :, CHUNK - 1:CHUNK].to_broadcast([P, GH * NCH, CHUNK]), ALU.subtract) \
                    .then_inc(*give("edin"))
                need("enb")
                k = ts[:, T_GK:T_GK + GH, :]
                dve.tensor_tensor(kinv[:], kinv[:], k, ALU.mult).then_inc(*give("gla_kinv"))
                softmax_in(1)
                split(O_TOK + 3, 1)
                need("gla_kinv")
                need("edec")
                dve.tensor_tensor(k, k, za[:], ALU.mult).then_inc(*give("gla_k"))
                softmax_out(1)
                split(O_TOK + 4, 0)
                attended_lo(0)
                split(O_TOK + 4, 1)
                split(O_TOK + 5, 0)
                attended_lo(1)
                for n in range(NCH - 1):
                    for gp in range(2):
                        f = ("ds", 2 * n + gp)
                        bank = ready(f)
                        if n == 0:
                            v = dve.tensor_copy(states[:, 0, 2 * gp:2 * gp + 2, :].rearrange("p g c -> p (g c)"), bank)
                        else:
                            in_sbuf(("ds", 2 * (n - 1) + gp))
                            for c in range(2):
                                g = 2 * gp + c
                                v = dve.scalar_tensor_tensor(states[:, n, g, :], states[:, n - 1, g, :],
                                                             decay[:, g, n:n + 1], bank[:, c * DV:(c + 1) * DV],
                                                             ALU.mult, ALU.add)
                        v.then_inc(*taken(f))
                gate(0)
                split(O_TOK + 5, 1)
                split(O_OUT, 0)
                gate(1)
                need("ossq")
                rstd_of(DV, TT * GH)
                for t in range(TT):
                    for gp in range(2):
                        f = ("o", 2 * t + gp)
                        for c in range(2):
                            g = 2 * gp + c
                            v = gg[:, t, g * DV:(g + 1) * DV]
                            i = dve.scalar_tensor_tensor(v, work[:, BANK[f][0], c * DV:(c + 1) * DV],
                                                         stat[:, 5, t * GH + g:t * GH + g + 1], v, ALU.mult, ALU.mult)
                        i.then_inc(*taken(f))
                split(O_OUT, 1)
                for i in range(4):
                    f = ("ot", i)
                    need("ot_hi", i + 1)
                    dve.tensor_tensor(oT[:, 2 * i:2 * i + 2, SEQ:2 * SEQ],
                                      work[:, BANK[f][0], :].rearrange("p (k q) -> p k q", q=SEQ),
                                      oT[:, 2 * i:2 * i + 2, 0:SEQ].bitcast(F32), ALU.subtract).then_inc(*taken(f))

                for j in range(4):
                    if j:
                        split(O_OUT + j, 1)
                    split(O_OUT + j + 1, 0)
                    need("ssq", S_OUT + j)
                    if j == 0:
                        dve.wait_ge(gpost_in, L * 32 + 16)
                    if j == 3:
                        mean_squares()
                    c = slice(512 * j, 512 * (j + 1))
                    weigh(facc[:, :, c], (acc[:, 2 * (j % 2):2 * (j % 2) + 2, :], gpost[:, c])) \
                        .then_inc(acc_free[j % 2], 1)
                for j in range(2):
                    dve.wait_ge(acc_free[j], L * PAIR_USES + (A_FFN + 1))

                newton(TT)
                for i in range(NORM + 3):
                    if i < NORM:
                        update(i, 1)
                    if i >= 3:
                        y_lo(i - 3, 2, KT)

                def quarter(q, first=False, last=False):
                    with dve.Fori(0, UP) as i:
                        i8 = (i + q * (UP + DN)) * 8
                        for half in range(2):
                            split(O_FFN + half, 1 - half, i8)
                            g = i * 2 + q * 8
                            dve.wait_ge(S["half"], g + at("half", 3 + 16 + half))
                            dve.tensor_tensor(u2[:, half], acc[:, 2 * half:2 * half + 2, 0:SEQ], scr[:, half], ALU.add) \
                                .then_inc(acc_free[half], 1)
                            dve.wait_ge(acc_free[half], i + q * (UP + DN // 2) + (L * PAIR_USES + (A_FFN + 2)))
                            dve.scalar_tensor_tensor(u2[:, half], u2[:, half], 0.0, u2[:, half], ALU.max, ALU.mult) \
                                .then_inc(S["squared"], 1)
                            dve.wait_ge(S["u_hi"], g + at("u_hi", 1 + half))
                            ut = bass.ds(i * 4 + 2 * half, 2)
                            dve.tensor_tensor(u[:, ut, SEQ:2 * SEQ], u2[:, half], u[:, ut, 0:SEQ].bitcast(F32),
                                              ALU.subtract).then_inc(S["u_lo"], 1)
                    if first:
                        pre_norm(S_PRE2)
                    with dve.Fori(0, DN // 2) as i:
                        i8 = (i * 2 + q * (UP + DN)) * 8
                        for j in range(2):
                            o = O_FFN + UP + j
                            split(o, 1, i8)
                            split(o + 1, 0, i8)
                            dve.wait_ge(block_done, done(i8 + (n0 + (8 * o + RAW - 1))))
                            c = bass.ds(i * 1024 + j * 512, 512)
                            for t in range(TT):
                                a, v, r2 = acc[:, 2 * j + t, :], facc[:, t, c], pre[:, 1, t:t + 1]
                                if first:
                                    v = dve.tensor_scalar(v, a, r2, None, ALU.mult)
                                else:
                                    v = dve.scalar_tensor_tensor(v, a, r2, v, ALU.mult, ALU.add)
                            v.then_inc(acc_free[j], 1)
                            if last:
                                dve.wait_ge(gpost_in, L * 32 + 32)
                                dve.wait_ge(S["ssq"], i * 2 + at("ssq", S_DOWN + j))
                                weigh(facc[:, :, c], (facc[:, :, c], gpost[:, c])).then_inc(weighed, 1)

                quarter(0, first=True)
                with dve.Fori(1, NQ - 1) as q:
                    quarter(q)
                quarter(NQ - 1, last=True)

                mean_squares()
                newton(TT)
                dve.wait_ge(weighed, L * DN + DN)
                for i in range(NORM):
                    update(i, 2)
                dve.wait_ge(S["h_done"], at("h_done", 2 * NORM + NORM))
            assert steps[0] == DVE_STEPS, steps
            for n in ("ms", "r0", "rstd", "zabs", "scaled", "zsc", "edin", "gla_q", "gla_kinv", "gla_k",
                      "relu_used", "masked", "negmax", "probs", "h_done", "gains", "gr_lo"):
                assert got[n] == PER[n], (n, got[n])


_INS = ["x", "positions", "norm_mix_pre", "w_in", "gla_wa2", "gla_ba", "gla_norm", "w_out", "norm_mix_post",
        "norm_ffn_pre", "w_up", "w_down", "norm_ffn_post"]


def kernel(**inputs):
    import concourse.bacc as bacc
    from concourse.bass_utils import run_bass_kernel_spmd

    nc = bacc.Bacc("TRN2", target_bir_lowering=False, num_devices=1)
    arrays = {f"in_{n}": np.ascontiguousarray(inputs[n]) for n in _INS}
    arrays["in_rope_constants"] = rope_constants()
    args = [nc.dram_tensor(n, a.shape, mybir.dt.from_np(a.dtype), kind="ExternalInput").ap()
            for n, a in arrays.items()]
    args.append(nc.dram_tensor("out", (1, SEQ, D), F32, kind="ExternalOutput").ap())
    trunk(nc, *args)
    return run_bass_kernel_spmd(nc, [arrays], core_ids=[0]).results[0]["out"]
```

```python
from contextlib import ExitStack

import numpy as np

import concourse.bass as bass
from concourse import mybir
from concourse.alu_op_type import AluOpType as ALU

F32 = mybir.dt.float32
F32R = mybir.dt.float32r
I32 = mybir.dt.int32
ACT = mybir.ActivationFunctionType
AX_X = mybir.AxisListType.X

P = 128
SEQ, D, DEPTH, D_FF = 256, 2048, 2, 8192
TT = SEQ // P
KT = D // P
GH, DK, DV, RANK, TAU, CHUNK = 4, 128, 256, 16, 16.0, 64
NCH = SEQ // CHUNK
AH, DH = 8, 128
IH, DI = 16, 64
TOPK = min(256, SEQ // 4)
ROPE_THETA, ROPE_FRACTION = 500000.0, 4
EPS, NEG = 1e-6, -1e30
TAKEN = -3e38
SPLITS = dict(gq=GH * DK, gk=GH * DK, gv=GH * DV, gg=GH * DV, gr=RANK, dq=AH * DH, dk=AH * DH,
              dv=AH * DH, iq=IH * DI, ik=DI, iw=IH)
COL, _c = {}, 0
for _n, _w in SPLITS.items():
    COL[_n] = _c
    _c += _w
D_IN = _c

BLK = 1024
RAW, HIS, QB = 8, 4, 4
MISC_W = DI + IH
O_T, O_TOK, O_OUT, O_FFN = 1, 9, 15, 19
NQ, UP, DN = 4, 4, 4
OCTETS = O_FFN + NQ * (UP + DN)
T_COLS = ["iq", "dq", "dk", "gq"]
TOK_COLS = ["dv", "gv", "gg"]
QT = D_FF // NQ // P
T_IQ, T_DQ, T_DK, T_GQ, T_GK = 0, 8, 16, 24, 28

A_MISC, A_T, A_TOK, A_OUT, A_FFN = -1, 0, 8, 11, 13
PAIR_USES = A_FFN + NQ * (UP + DN // 2)

FILLS = [(name, i) for name, n in (
    ("norm1", 8), ("rb", 1), ("z", 2), ("iw", 1), ("log0", 4), ("log1", 8), ("sc0", 2), ("pt0", 2),
    ("sc1", 4), ("pv0", 2), ("pt1", 4), ("kd", 2), ("at", 1), ("pv1", 2), ("ds", 6), ("o", 4), ("ot", 4),
    ("norm2", 8)) for i in range(n)]
BANKS = 4
BANK, USES = {}, [0] * BANKS
for _i, _f in enumerate(FILLS):
    BANK[_f] = (_i % BANKS, USES[_i % BANKS])
    USES[_i % BANKS] += 1

SET_DVE_ARGS, SET_DVE_GAINS = 11, 12
NORM = 8
S_PRE, S_OUT, S_PRE2, S_DOWN = 1, 2, 6, 7

PER = dict(
    gr_hi=1, gr_lo=1,
    ssq=10,
    ms=2,
    r0=5,
    rstd=2, post_rstd=2,
    posted=NORM,
    y_hi=2 * NORM,
    half=50,
    rot=52,
    scaled=1,
    zabs=1, zl=1, zsc=1,
    eb=1, enb=1, edin=1, edec=1,
    gla_q=1, gla_kinv=1, gla_k=1,
    relu_used=12,
    causal=2, masked=2, allowed=2,
    negmax=2, expd=2, probs=2,
    pv_hi=4, ot_hi=4,
    at_masked=2,
    gate_e=2, ossq=4,
    squared=32, u_hi=32, u_lo=32)
DVE_STEPS, ACT_STEPS = 68, 10
OUT_ROWS = [8, 10, 12, 14, 0, 2, 4, 6]


def rope_constants():
    c = np.zeros((P, 4), np.float32)
    for col, dim in ((0, DH), (2, DI)):
        r = dim // ROPE_FRACTION
        inv = np.float32(ROPE_THETA) ** (-(np.arange(0, r, 2, dtype=np.float32) / np.float32(r)))
        for p in range(P):
            d = p % dim
            if d < r:
                c[p, col] = inv[d % (r // 2)]
                c[p, col + 1] = -1.0 if d < r // 2 else 1.0
    return c


def swap_mask(half):
    return [i + half if i < half else i - half if i < 2 * half else i for i in range(32)]


def trunk(nc, x, positions, norm_mix_pre, w_in, gla_wa2, gla_ba, gla_norm, w_out, norm_mix_post,
          norm_ffn_pre, w_up, w_down, norm_ffn_post, rope_c, out):
    with ExitStack() as ctx:
        top = [-(-nc.sbuf_base // 64) * 64]

        def place(name, shape, dt=F32, at=None):
            where = top[0] if at is None else at
            if at is None:
                top[0] += -(-int(np.prod(shape[1:])) * 4 // 32) * 32
            return nc.alloc_sbuf_tensor_at(name, shape, dt, offset=where)

        KB = 1024
        h = place("h", [P, TT, D])
        Y = top[0]
        y = place("y", [P, KT, 2 * SEQ], F32R)
        squares = place("squares", [P, TT, D], at=Y)
        LR = top[0]
        raw = place("raw_ring", [P, RAW, BLK])
        lo = place("lo_ring", [P, RAW, BLK], F32R, at=LR)
        hi = place("hi_ring", [P, HIS, BLK], F32R)
        U = top[0]
        u = place("u", [P, QT, 2 * SEQ], F32R)
        oT = place("oT", [P, KT, 2 * SEQ], F32R, at=U)
        probs = place("probs", [P, AH, SEQ], at=U)
        rb = place("rb", [P, SEQ], at=U)
        rot_k = place("rot_k", [P, 2, SEQ], at=U + 8 * KB)
        kinv = place("kinv", [P, GH, SEQ], at=U + 8 * KB)
        za = place("za", [P, GH, SEQ], at=U + 12 * KB)
        at_sb = place("at_sb", [P, TT, GH, CHUNK], at=U + 12 * KB)
        relus = place("relus", [P, BANKS, 2 * SEQ], at=U + 16 * KB)
        swapped = place("swapped", [P, 2, SEQ], at=U + 24 * KB)
        fresh = place("fresh", [P, 2, 2, SEQ], at=U + 26 * KB)
        FA = top[0]
        facc = place("facc", [P, TT, D])
        dv = place("dv", [P, TT, AH * DH], at=FA)
        gv = place("gv", [P, TT, GH * DV], at=FA + 8 * KB)
        TS = top[0]
        ts = place("ts", [P, 32, SEQ])
        ptT = place("ptT", [P, AH, TT, P], at=TS)
        states = place("states", [P, NCH - 1, GH, DV], at=TS + 8 * KB)
        kd = place("kd", [P, TT, GH * DK], at=TS + 20 * KB)
        gpost = place("gpost", [P, D], at=TS)
        u2 = place("u2", [P, 2, 2, SEQ], at=TS + 8 * KB)
        gains_in = place("gains_in", [P, P], at=TS)
        gg = place("gg", [P, TT, GH * DV])
        misc = place("misc", [P, SEQ])
        GR = top[0]
        gr = place("gr", [P, SEQ])
        w_gr = place("w_gr", [P, KT, RANK], at=GR)
        ikz = place("ikz", [P, 2, SEQ])
        rot = place("rot", [P, 2, 2, SEQ])
        rot_a, rot_i = rot[:, :, 0, :], rot[:, :, 1, :]
        ident = place("ident", [P, P])
        within = place("within", [P, SEQ])
        gains_all = place("gains_all", [P, (DEPTH + 1) * (2 * KT + GH)])
        gains = place("gains", [P, 2 * KT + GH])
        wa2 = place("wa2", [P, GH * DK])
        gnorm = place("gnorm", [P, DV])
        score = place("score", [P, TT, SEQ])
        scr = place("scr", [P, 2, 2, SEQ])
        ZB = top[0]
        zb = place("zb", [P, GH, SEQ])
        gr_hi = place("gr_hi", [P, KT, RANK], F32R, at=ZB)
        gr_lo = place("gr_lo", [P, KT, RANK], F32R, at=ZB + KB)
        iw = place("iw", [P, TT, IH])
        top8 = place("top8", [P, TT, 8])
        decay = place("decay", [P, GH, NCH])
        stat = place("stat", [P, 6, 8])
        pre = place("pre", [P, 3, TT])
        smax = place("smax", [P, 3, AH])
        eps_c, one_c = place("eps_c", [P, 1]), place("one_c", [P, 1])
        rc = place("rc", [P, 4])
        assert top[0] <= nc.sbuf_usable_end, top[0] - nc.sbuf_usable_end
        scr_gate = place("scr_gate", [P, TT, 2, 512], at=U)
        pos_i = place("pos_i", [P, SEQ], I32, at=U)
        pos_f = place("pos_f", [P, SEQ], at=U + KB)
        angle, co_angle, turns = (place(n, [P, 2, SEQ], at=U + (2 + 2 * i) * KB)
                                  for i, n in enumerate(("angle", "co_angle", "turns")))

        acc = ctx.enter_context(nc.psum_tensor("acc", [P, 4, 512], F32))
        work = ctx.enter_context(nc.psum_tensor("work", [P, BANKS, 512], F32))

        def sem(name):
            return ctx.enter_context(nc.semaphore(name))

        landed = [sem(f"landed{i}") for i in range(RAW)]
        block_done = sem("block_done")
        hi_done, lo_done = sem("hi_done"), sem("lo_done")
        acc_free = [sem(f"acc_free{i}") for i in range(2)]
        bank_ready = [sem(f"bank_ready{i}") for i in range(BANKS)]
        bank_free = [sem(f"bank_free{i}") for i in range(BANKS)]
        S = {n: sem("s_" + n) for n in PER}
        wa2_in, gnorm_in, gpost_in, w_gr_in = (sem(n) for n in ("wa2_in", "gnorm_in", "gpost_in", "w_gr_in"))
        dve_step, act_step = sem("dve_step"), sem("act_step")
        weighed = sem("weighed")
        dve_stood, pool_stood, pe_stood = sem("dve_stood"), sem("pool_stood"), sem("pe_stood")
        gains_dma, pos_in, rc_in, set_pool, consts, set_dve, set_act, set_pe, stored = (sem(n) for n in (
            "gains_dma", "pos_in", "rc_in", "set_pool", "consts", "set_dve", "set_act", "set_pe", "stored"))
        h_done = [sem(f"h_done{i}") for i in range(2)]
        h_dma = [sem(f"h_dma{i}") for i in range(2)]
        GAINS_DMAS, CONSTS = 3, 5
        NG = 2 * KT + GH

        w_in_v = w_in.rearrange("l (k p) c -> p l k c", p=P)
        w_out_v = w_out.rearrange("l (k p) c -> p l k c", p=P)
        w_up_v = w_up.rearrange("l (k p) c -> p l k c", p=P)
        w_dn_v = w_down.rearrange("l (k p) c -> p l k c", p=P)

        def used_misc(ring, slot):
            return ring[:, slot, :].rearrange("p (k c) -> p k c", k=2)[:, :, 512 - MISC_W:512]

        def done(number):
            return number + (1 + RAW)

        def pair_free(L, pair, use):
            return L * (PAIR_USES + pair) + (pair + use + 1)

        def h_count(L, stage, i=NORM - 1):
            return L * NORM + (stage * NORM // 2 + i // 2 + 1)

        block = ctx.enter_context(nc.Block())

        @block.sync
        def _(sp):
            def load(slot, number, src, k, c):
                sp.wait_ge(block_done, number + 1)
                sp.dma_start(raw[:, slot, 0:k * c].rearrange("p (k c) -> p k c", k=k),
                             src.rearrange("p l k c -> p (l k) c")).then_inc(landed[slot], 16)

            def misc_quad(L, number, half):
                w = MISC_W if half else 512
                for j in range(half * QB, half * QB + QB):
                    load(j, number + j, w_in_v[:, bass.ds(L, 1), 2 * j:2 * j + 2, D_IN - w:D_IN], 2, w)

            def feature_octet(L, number, w, col):
                for j in range(RAW):
                    half, b = j // QB, j % QB
                    load(j, number + j, w[:, bass.ds(L, 1), 4 * b:4 * b + 4, bass.ds(col + 256 * half, 256)], 4, 256)

            def token_octet(L, number, w, rows, col):
                for j in range(RAW):
                    load(j, number + j, w[:, bass.ds(L, 1), bass.ds(rows[j], 2), bass.ds(col, 512)], 2, 512)

            sp.dma_start(rc[:], rope_c).then_inc(rc_in, 16)
            straight = [2 * b for b in range(RAW)]
            for j in range(QB):
                sp.dma_start(used_misc(raw, j), w_in_v[:, 0, 2 * j:2 * j + 2, D_IN - MISC_W:D_IN]) \
                    .then_inc(landed[j], 16)
            with sp.Fori(0, DEPTH) as L:
                n0 = L * (8 * OCTETS)
                sp.dma_start(w_gr[:], w_in_v[:, bass.ds(L, 1), :, COL["gr"]:COL["gr"] + RANK]
                             .rearrange("p l k c -> p (l k) c")).then_inc(w_gr_in, 16)
                misc_quad(L, n0, 1)
                for g, name in enumerate(T_COLS):
                    with sp.Fori(0, 2) as i:
                        feature_octet(L, n0 + i * 8 + 8 * (O_T + 2 * g), w_in_v, i * 512 + COL[name])
                for g, name in enumerate(TOK_COLS):
                    with sp.Fori(0, 2) as i:
                        token_octet(L, n0 + i * 8 + 8 * (O_TOK + 2 * g), w_in_v, straight, i * 512 + COL[name])
                with sp.Fori(0, 4) as i:
                    token_octet(L, n0 + i * 8 + 8 * O_OUT, w_out_v, OUT_ROWS, i * 512)
                with sp.Fori(0, NQ) as q:
                    nq = n0 + q * (8 * (UP + DN)) + 8 * O_FFN
                    with sp.Fori(0, UP) as i:
                        feature_octet(L, nq + i * 8, w_up_v, q * (QT * P) + i * 512)
                    with sp.Fori(0, DN) as i:
                        token_octet(L, nq + i * 8 + 8 * UP, w_dn_v, [q * QT + 2 * b for b in range(RAW)], i * 512)
                assert DEPTH == 2
                misc_quad(L * -1 + (DEPTH - 1), n0 + 8 * OCTETS, 0)
            for i in range(NORM):
                c = slice(i * D // NORM, (i + 1) * D // NORM)
                sp.wait_ge(h_done[i % 2], h_count(DEPTH, 0, i))
                sp.dma_start(out[0].rearrange("(t p) d -> p t d", p=P)[:, :, c], h[:, :, c]).then_inc(stored, 16)
            sp.wait_ge(stored, NORM * 16)

        @block.gpsimd
        def _(pool):
            got = dict.fromkeys(PER, 0)

            def wait(s, value):
                pool.wait_ge(s, value)
                pool.sem_inc(pool_stood, 1)

            pool.dma_start(pos_i[:], positions[0].partition_broadcast(P)).then_inc(pos_in, 16)
            pool.memset(ident[:], 0.0).then_inc(set_pool, 1)
            pool.memset(within[:], 1.0).then_inc(set_pool, 1)
            pool.memset(ikz[:], 0.0).then_inc(consts, 1)
            pool.memset(eps_c[:], EPS).then_inc(consts, 1)
            pool.memset(one_c[:], 1.0).then_inc(consts, 1)
            for s in acc_free + bank_free:
                pool.sem_inc(s, 1)
            pool.sem_inc(block_done, RAW)
            pool.wait_ge(set_pool, 2)
            pool.affine_select(out=ident[:], in_=ident[:], compare_op=ALU.not_equal, fill=1.0, base=0,
                               pattern=[[-1, P]], channel_multiplier=1).then_inc(consts, 1)
            pool.memset(within[:].rearrange("p (n c) -> p n c", c=CHUNK)[:, :, 0:1], 0.0).then_inc(consts, 1)

            for i in range(2):
                pool.wait_ge(h_dma[i], 16)
                for s in h_done:
                    pool.sem_inc(s, NORM // 4)

            with pool.Fori(0, DEPTH) as L:
                def at(name, n):
                    return L * PER[name] + n

                def give(name):
                    got[name] += 1
                    return S[name], 1

                def ready(f):
                    b, n = BANK[f]
                    wait(bank_ready[b], L * USES[b] + n + 1)

                def row(src):
                    return src[bass.ds(L, 1)].rearrange("l c -> (l c)").partition_broadcast(P)

                def hide_future(t):
                    v = score[:, t, t * P:(t + 1) * P]
                    return pool.affine_select(out=v, in_=v, compare_op=ALU.is_ge, fill=NEG, base=0,
                                              pattern=[[-1, P]], channel_multiplier=1)

                def update(n):
                    for i in range(1, NORM, 2):
                        c = slice(i * D // NORM, (i + 1) * D // NORM)
                        pool.wait_ge(S["posted"], at("posted", (n * NORM + i) // 2 + 1))
                        pool.tensor_tensor(h[:, :, c], h[:, :, c], facc[:, :, c], ALU.add).then_inc(h_done[1], 1)

                pool.dma_start(wa2[0:RANK, :], gla_wa2[bass.ds(L, 1)].rearrange("l r c -> (l r) c")) \
                    .then_inc(wa2_in, 16)
                pool.dma_start(gnorm[:], row(gla_norm)).then_inc(gnorm_in, 16)
                for t in range(TT):
                    wait(S["relu_used"], at("relu_used", 4 + 8 * t))
                    hide_future(t).then_inc(*give("causal"))
                for t in range(TT):
                    wait(S["masked"], at("masked", t + 1))
                    hide_future(t).then_inc(*give("allowed"))
                b_at, n_at = BANK["at", 0]
                wait(bank_free[b_at], L * USES[b_at] + n_at + 2)
                for c in range(2):
                    v = at_sb[c * CHUNK:(c + 1) * CHUNK].rearrange("p t g c -> p (t g) c")
                    pool.affine_select(out=v, in_=v, compare_op=ALU.is_ge, fill=0.0, base=0,
                                       pattern=[[0, TT * GH], [1, CHUNK]], channel_multiplier=-1) \
                        .then_inc(*give("at_masked"))
                ready(("pv1", 1))
                pool.dma_start(gpost[:], row(norm_mix_post)).then_inc(gpost_in, 16)
                update(0)
                wait(h_done[0], h_count(L, 1))
                pool.dma_start(gpost[:], row(norm_ffn_post)).then_inc(gpost_in, 16)
                update(1)
            for n in ("causal", "allowed", "at_masked"):
                assert got[n] == PER[n], (n, got[n])

        @block.scalar
        def _(act):
            got = dict.fromkeys(PER, 0)
            steps = [0]

            def split_hi(number, slot0, landed_n, n=BLK, blocks=range(QB)):
                for b in blocks:
                    act.wait_ge(landed[slot0 + b], landed_n)
                    act.wait_ge(block_done, number + (b + 1 + RAW - HIS))
                    act.activation(hi[:, b, 0:n], raw[:, slot0 + b, 0:n], ACT.Copy).then_inc(hi_done, 1)

            for row, src, n in ((0, norm_mix_pre, KT), (DEPTH * KT, norm_ffn_pre, KT), (2 * DEPTH * KT, gla_ba, GH)):
                act.dma_start(gains_in[row:row + DEPTH * n, :],
                              src.rearrange("l (k p) -> (l k) p", p=P)).then_inc(gains_dma, 16)
            for i in range(2):
                c = slice(i * D // 2, (i + 1) * D // 2)
                act.dma_start(h[:, :, c], x[0].rearrange("(t p) d -> p t d", p=P)[:, :, c]).then_inc(h_dma[i], 16)
            for b in range(QB):
                act.wait_ge(landed[b], 16)
                act.activation(used_misc(hi, b), used_misc(raw, b), ACT.Copy).then_inc(hi_done, 1)
            act.wait_ge(set_dve, SET_DVE_ARGS)
            for i, arg in ((1, angle), (0, co_angle)):
                act.activation(rot[:, i], arg[:], ACT.Sin).then_inc(set_act, 1)
            act.wait_ge(consts, CONSTS)
            act.preload_act_table_set("natural_log_exp_and_others")

            with act.Fori(0, DEPTH) as L:
                n0, l0 = L * (8 * OCTETS), L * (16 * OCTETS)

                def at(name, n):
                    return L * PER[name] + n

                def give(name):
                    got[name] += 1
                    return S[name], 1

                def step(a):
                    steps[0] += 1
                    a.then_inc(act_step, 1)
                    act.wait_ge(act_step, L * ACT_STEPS + steps[0])

                def split(o, half, i8=0, i16=0, n=BLK):
                    split_hi(n0 + i8 + (8 * o + half * QB), half * QB, l0 + i16 + 16 * (o + 1), n)

                def split_block(o, half, b, n=BLK):
                    split_hi(n0 + (8 * o + half * QB), half * QB, l0 + 16 * (o + 1), n, [b])

                def ready(f):
                    b, n = BANK[f]
                    act.wait_ge(bank_ready[b], L * USES[b] + n + 1)
                    return work[:, b, :]

                def taken(f):
                    return bank_free[BANK[f][0]], 1

                def rsqrt(src, cols, scale=1.0, bias=0.0):
                    step(act.activation(stat[:, 2, 0:cols], src, ACT.Ln, scale=scale, bias=bias))
                    act.activation(stat[:, 3, 0:cols], stat[:, 2, 0:cols], ACT.Exp, scale=-0.5) \
                        .then_inc(*give("r0"))

                def pre_norm():
                    for t in range(TT):
                        a = act.activation(facc[:, t, :], h[:, t, :], ACT.Square, accum_out=stat[:, 0, t:t + 1])
                    a.then_inc(*give("ssq"))
                    act.wait_ge(S["ssq"], at("ssq", got["ssq"]))
                    rsqrt(stat[:, 0, 0:TT], TT, 1.0 / D, eps_c[:, 0:1])

                def post_norm(n):
                    act.wait_ge(S["ms"], at("ms", n))
                    rsqrt(stat[:, 1, 0:TT], TT)
                    act.wait_ge(S["post_rstd"], at("post_rstd", n))

                def scale_block(i):
                    c = slice(i * D // NORM, (i + 1) * D // NORM)
                    for t in range(TT):
                        a = act.activation(facc[:, t, c], facc[:, t, c], ACT.Copy, scale=stat[:, 5, t:t + 1])
                    a.then_inc(*give("posted"))

                def y_hi(i, which, g0):
                    bank = ready((f"norm{which}", i))
                    for c in range(2):
                        k = 2 * i + c
                        a = act.activation(y[:, k, 0:SEQ], bank[:, c * SEQ:(c + 1) * SEQ], ACT.Copy,
                                           scale=gains[:, g0 + k:g0 + k + 1])
                    a.then_inc(*give("y_hi"))

                def block_squares(c, src, block):
                    for t in range(TT):
                        a = act.activation(squares[:, t, c], src[:, t, :], ACT.Square, accum_out=block(t))
                    return a

                def second_half(pair, number):
                    act.wait_ge(block_done, done(number))
                    act.activation(scr[:, pair], acc[:, 2 * pair:2 * pair + 2, SEQ:2 * SEQ], ACT.Copy) \
                        .then_inc(S["half"], 1)

                def token_out(j, dst):
                    act.wait_ge(block_done, done(n0 + (8 * (O_TOK + j) + RAW - 1)))
                    pair = j % 2
                    for t in range(TT):
                        a = act.activation(dst[:, t, :], acc[:, 2 * pair + t, :], ACT.Copy, scale=pre[:, 0, t:t + 1])
                    a.then_inc(acc_free[pair], 1)

                act.wait_ge(w_gr_in, L * 16 + 16)
                act.activation(gr_hi[:], w_gr[:], ACT.Copy).then_inc(*give("gr_hi"))
                for i in range(NORM):
                    if i >= NORM - QB:
                        split_block(0, 1, i - (NORM - QB), 2 * MISC_W)
                    y_hi(i, 1, 0)
                for b in range(QB - 1):
                    split_block(O_T, 0, b)
                act.wait_ge(block_done, done(n0 + (RAW - 1)))
                for i, rows in enumerate((MISC_W, RANK)):
                    act.activation(scr[0:rows, 0, i, :], acc[0:rows, 2 + i, SEQ:2 * SEQ], ACT.Copy) \
                        .then_inc(*give("half"))
                split_block(O_T, 0, QB - 1)

                def features(g):
                    with act.Fori(0, 2) as i:
                        o = O_T + 2 * g
                        for half in range(2):
                            split(o + half, 1 - half, i * 8, i * 16)
                            second_half(half, n0 + i * 8 + (8 * o + half * QB + QB - 1))

                for s in h_done:
                    act.wait_ge(s, h_count(L, 0))
                pre_norm()
                act.wait_ge(acc_free[1], pair_free(L, 1, A_MISC) + 1)
                features(0)
                features(1)
                features(2)
                for i in range(2):
                    bank = ready(("z", i))
                    for c in range(2):
                        g = 2 * i + c
                        a = act.activation(za[:, g, :], bank[:, c * SEQ:(c + 1) * SEQ], ACT.Identity,
                                           bias=gains[:, 2 * KT + g:2 * KT + g + 1])
                    a.then_inc(*taken(("z", i)))
                features(3)
                act.wait_ge(S["zabs"], at("zabs", 1))
                step(act.activation(zb[:], zb[:], ACT.Exp, scale=-1.0))
                act.activation(zb[:], zb[:], ACT.Ln, bias=one_c[:, 0:1]).then_inc(*give("zl"))
                for n, f in enumerate([("log0", i) for i in range(4)] + [("log1", i) for i in range(8)]):
                    bank = ready(f)
                    if n >= BANKS:
                        act.wait_ge(S["relu_used"], at("relu_used", n - BANKS + 1))
                    act.activation(relus[:, n % BANKS, :], bank, ACT.Relu).then_inc(*taken(f))

                def exps(t):
                    act.wait_ge(S["negmax"], at("negmax", t + 1))
                    for a in range(AH):
                        v = probs[:, a, 0:(t + 1) * P]
                        e = act.activation(v, v, ACT.Exp, bias=smax[:, 0, a:a + 1], accum_out=smax[:, 1, a:a + 1])
                    e.then_inc(*give("expd"))

                def transposed_probs(t):
                    for i in range((t + 1) * 2):
                        f = (f"pt{t}", i)
                        if t == 0:
                            dst = ptT[:, 4 * i:4 * i + 4, 0, :]
                        else:
                            dst = ptT[:, 2 * i:2 * i + 2, :, :].rearrange("p a j q -> p (a j) q")
                        act.activation(dst, ready(f).rearrange("p (a q) -> p a q", q=P), ACT.Copy) \
                            .then_inc(*taken(f))

                def attended(t):
                    for i in range(2):
                        k0 = KT // 2 + 4 * i
                        act.activation(oT[:, k0:k0 + 4, t * P:(t + 1) * P],
                                       ready((f"pv{t}", i)).rearrange("p (a q) -> p a q", q=P), ACT.Copy) \
                            .then_inc(*give("pv_hi"))

                def gate_exp(j):
                    act.wait_ge(acc_free[j], pair_free(L, j, A_TOK + 2) + 1)
                    v = scr_gate[:, :, j, :]
                    step(act.activation(v, gg[:, :, 512 * j:512 * j + 512], ACT.Exp, scale=-1.0))
                    step(act.activation(v, v, ACT.Ln, bias=one_c[:, 0:1]))
                    act.activation(v, v, ACT.Exp, scale=-1.0).then_inc(*give("gate_e"))

                split(O_TOK, 1)
                split(O_TOK + 1, 0)
                act.wait_ge(S["rstd"], at("rstd", 1))
                token_out(0, dv[:, :, 0:512])
                split(O_TOK + 1, 1)
                split(O_TOK + 2, 0)
                token_out(1, dv[:, :, 512:1024])
                exps(0)
                split(O_TOK + 2, 1)
                act.wait_ge(S["zsc"], at("zsc", 1))
                act.activation(za[:], zb[:], ACT.Exp, scale=1.0 / TAU).then_inc(*give("eb"))
                act.activation(kinv[:], zb[:], ACT.Exp, scale=-1.0 / TAU).then_inc(*give("enb"))
                split(O_TOK + 3, 0)
                token_out(2, gv[:, :, 0:512])
                transposed_probs(0)
                split(O_TOK + 3, 1)
                exps(1)
                act.wait_ge(S["edin"], at("edin", 1))
                act.activation(za[:], za[:], ACT.Exp, scale=-1.0 / TAU).then_inc(*give("edec"))
                split(O_TOK + 4, 0)
                token_out(3, gv[:, :, 512:1024])
                attended(0)
                transposed_probs(1)
                for t in range(TT):
                    act.activation(kd[:, t, :], ready(("kd", t)), ACT.Copy).then_inc(*taken(("kd", t)))
                act.activation(at_sb[:].rearrange("p t g c -> p (t g c)"), ready(("at", 0)), ACT.Copy) \
                    .then_inc(*taken(("at", 0)))
                split(O_TOK + 4, 1)
                split(O_TOK + 5, 0)
                token_out(4, gg[:, :, 0:512])
                attended(1)
                gate_exp(0)
                split(O_TOK + 5, 1)
                split(O_OUT, 0)
                token_out(5, gg[:, :, 512:1024])
                gate_exp(1)
                for t in range(TT):
                    for gp in range(2):
                        bank = ready(("o", 2 * t + gp))
                        for c in range(2):
                            g = t * GH + 2 * gp + c
                            a = act.activation(squares[:, 0, g * DV:(g + 1) * DV], bank[:, c * DV:(c + 1) * DV], ACT.Square,
                                               accum_out=stat[:, 0, g:g + 1])
                        a.then_inc(*give("ossq"))
                act.wait_ge(S["ossq"], at("ossq", PER["ossq"]))
                rsqrt(stat[:, 0, 0:TT * GH], TT * GH, 1.0 / DV, eps_c[:, 0:1])
                for b in range(QB - 1):
                    split_block(O_OUT, 1, b)
                for i in range(4):
                    act.activation(oT[:, 2 * i:2 * i + 2, 0:SEQ],
                                   ready(("ot", i)).rearrange("p (k q) -> p k q", q=SEQ), ACT.Copy) \
                        .then_inc(*give("ot_hi"))
                split_block(O_OUT, 1, QB - 1)

                for j in range(4):
                    if j:
                        split(O_OUT + j, 1)
                    for b in range(QB if j < 3 else QB - 1):
                        split_block(O_OUT + j + 1, 0, b)
                    act.wait_ge(block_done, done(n0 + (8 * (O_OUT + j) + RAW - 1)))
                    block_squares(slice(512 * j, 512 * (j + 1)), acc[:, 2 * (j % 2):2 * (j % 2) + 2, :],
                                  lambda t: stat[:, 0, 4 * t + j:4 * t + j + 1]).then_inc(*give("ssq"))

                post_norm(1)
                for i in range(1, NORM - 2, 2):
                    scale_block(i)
                for i in range(NORM):
                    y_hi(i, 2, KT)
                    if i == 1:
                        act.wait_ge(acc_free[1], pair_free(L, 1, A_OUT + 1) + 1)
                        scale_block(NORM - 1)
                    if i == 4:
                        split_block(O_FFN, 0, QB - 1)

                def down(q, i, j):
                    i8 = (i * 2 + q * (UP + DN)) * 8
                    split(O_FFN + UP + j, 1, i8, i8 * 2)
                    split(O_FFN + UP + j + 1, 0, i8, i8 * 2)

                def quarter(q, first=False, last=False):
                    with act.Fori(0, UP) as i:
                        i8 = (i + q * (UP + DN)) * 8
                        for half in range(2):
                            split(O_FFN + half, 1 - half, i8, i8 * 2)
                            second_half(half, n0 + i8 + (8 * O_FFN + half * QB + QB - 1))
                            act.wait_ge(S["squared"], i * 2 + q * 8 + at("squared", 1 + half))
                            act.activation(u[:, bass.ds(i * 4 + 2 * half, 2), 0:SEQ], u2[:, half], ACT.Copy) \
                                .then_inc(S["u_hi"], 1)
                    if first:
                        for s in h_done:
                            act.wait_ge(s, h_count(L, 1))
                        pre_norm()
                    if not last:
                        with act.Fori(0, DN // 2) as i:
                            for j in range(2):
                                down(q, i, j)

                quarter(0, first=True)
                with act.Fori(1, NQ - 1) as q:
                    quarter(q)
                quarter(NQ - 1, last=True)
                for j in range(DN):
                    down(NQ - 1, j // 2, j % 2)
                    act.wait_ge(acc_free[j % 2], pair_free(L, j % 2, PAIR_USES - DN // 2 + j // 2) + 1)
                    c = slice(512 * j, 512 * (j + 1))
                    block_squares(c, facc[:, :, c], lambda t: stat[:, 0, 4 * t + j:4 * t + j + 1]) \
                        .then_inc(*give("ssq"))

                post_norm(2)
                for i in range(1, NORM - 2, 2):
                    scale_block(i)
                act.wait_ge(weighed, L * DN + DN)
                scale_block(NORM - 1)
            assert steps[0] == ACT_STEPS, steps
            for n in ("gr_hi", "y_hi", "r0", "zl", "eb", "enb", "edec", "expd", "pv_hi", "ossq",
                      "ot_hi", "gate_e"):
                assert got[n] == PER[n], (n, got[n])

        @block.tensor
        def _(pe):
            pe.wait_ge(consts, CONSTS)
            pe.wait_ge(gains_dma, 16 * GAINS_DMAS)
            pe.transpose(work[:, 0, 0:DEPTH * NG], gains_in[0:DEPTH * NG, :], ident[0:DEPTH * NG, 0:DEPTH * NG]) \
                .then_inc(set_pe, 1)
            pe.wait_ge(set_dve, SET_DVE_GAINS)

            with pe.Fori(0, DEPTH) as L:
                n0 = L * (8 * OCTETS)

                def at(name, n):
                    return L * PER[name] + n

                def need(name, n=None):
                    pe.wait_ge(S[name], at(name, PER[name] if n is None else n))

                def fill(f):
                    b, n = BANK[f]
                    pe.wait_ge(bank_free[b], L * USES[b] + n + 1)
                    return work[:, b, :]

                def filled(f):
                    return bank_ready[BANK[f][0]], 1

                def taken(f):
                    b, n = BANK[f]
                    pe.wait_ge(bank_free[b], L * USES[b] + n + 2)

                def norm_transposes(which, chunks):
                    for i in chunks:
                        bank = fill((f"norm{which}", i))
                        pe.wait_ge(h_done[i % 2], h_count(L, which - 1, i))
                        for c in range(2):
                            for t in range(TT):
                                k = 2 * i + c
                                mm = pe.transpose(bank[:, c * SEQ + t * P:c * SEQ + (t + 1) * P],
                                                  h[:, t, k * P:(k + 1) * P], ident[:])
                        mm.then_inc(*filled((f"norm{which}", i)))

                def feature_products(bank, w_lo, w_hi, k):
                    last = k == KT - 1
                    if k == 0:
                        pe.matmul(bank, w_hi, y[:, k, :], start=True, stop=False)
                        return pe.matmul(bank[:, 0:SEQ], w_lo, y[:, k, 0:SEQ], start=False, stop=False)
                    pe.matmul(bank[:, 0:SEQ], w_lo, y[:, k, 0:SEQ], start=False, stop=False)
                    return pe.matmul(bank, w_hi, y[:, k, :], start=False, stop=last)

                def feature_octet(number, uses, before=None):
                    for half in range(2):
                        pe.wait_ge(acc_free[half], uses + pair_free(L, half, 0))
                        for b in range(QB):
                            j = half * QB + b
                            if before and half == 0:
                                before(b)
                            pe.wait_ge(lo_done, number + (j + 1))
                            lo_b = lo[:, j, :].rearrange("p (k c) -> p k c", k=4)
                            hi_b = hi[:, b, :].rearrange("p (k c) -> p k c", k=4)
                            for kk in range(4):
                                for c in range(2):
                                    mm = feature_products(acc[:, 2 * half + c, :], lo_b[:, kk, c * P:(c + 1) * P],
                                                          hi_b[:, kk, c * P:(c + 1) * P], 4 * b + kk)
                            mm.then_inc(block_done, 1)

                def token_octet(number, pair, uses, xs, order, before=None):
                    pe.wait_ge(acc_free[pair], uses + pair_free(L, pair, 0))
                    for j in range(RAW):
                        if before:
                            before(j)
                        pe.wait_ge(lo_done, number + (j + 1))
                        lo_b = lo[:, j, :].rearrange("p (k c) -> p k c", k=2)
                        hi_b = hi[:, j % HIS, :].rearrange("p (k c) -> p k c", k=2)
                        for kk in range(2):
                            k = order[j] + kk
                            first, last = j == 0 and kk == 0, j == RAW - 1 and kk == 1
                            for t in range(TT):
                                x_hi, x_lo = xs[:, k, t * P:(t + 1) * P], xs[:, k, SEQ + t * P:SEQ + (t + 1) * P]
                                a = acc[:, 2 * pair + t, :]
                                pe.matmul(a, x_hi, lo_b[:, kk, :], start=first, stop=False)
                                pe.matmul(a, x_hi, hi_b[:, kk, :], start=False, stop=False)
                                mm = pe.matmul(a, x_lo, hi_b[:, kk, :], start=False, stop=last)
                        mm.then_inc(block_done, 1)

                for j in range(RAW):
                    norm_transposes(1, range(BANKS) if j == 0 else [j + BANKS - 1] if j + BANKS - 1 < NORM else [])
                    if j == 0:
                        need("gr_lo")
                        pe.wait_ge(acc_free[1], pair_free(L, 1, A_MISC))
                    taken(("norm1", j))
                    pe.wait_ge(lo_done, n0 + (j + 1))
                    w = 512 if j < QB else MISC_W
                    lo_b = lo[:, j, 0:2 * w].rearrange("p (k c) -> p k c", k=2)[:, :, w - MISC_W:w]
                    hi_b = hi[:, j % HIS, 0:2 * w].rearrange("p (k c) -> p k c", k=2)[:, :, w - MISC_W:w]
                    for kk in range(2):
                        k = 2 * j + kk
                        feature_products(acc[0:RANK, 3, :], gr_lo[:, k, :], gr_hi[:, k, :], k)
                        mm = feature_products(acc[0:MISC_W, 2, :], lo_b[:, kk, :], hi_b[:, kk, :], k)
                    mm.then_inc(block_done, 1)

                def features(g):
                    with pe.Fori(0, 2) as i:
                        feature_octet(n0 + i * 8 + 8 * (O_T + 2 * g), i + (A_T + 2 * g))

                features(0)
                features(1)
                rb_bank = fill(("rb", 0))
                need("rstd", 1)
                for t in range(TT):
                    mm = pe.transpose(rb_bank[:, t * P:(t + 1) * P], pre[:, 0, t:t + 1].to_broadcast([P, P]), ident[:])
                mm.then_inc(*filled(("rb", 0)))
                features(2)
                need("scaled")
                pe.wait_ge(wa2_in, L * 16 + 16)
                iw_bank = fill(("iw", 0))
                for i in range(2):
                    bank = fill(("z", i))
                    for c in range(2):
                        g = 2 * i + c
                        mm = pe.matmul(bank[:, c * SEQ:(c + 1) * SEQ], wa2[0:RANK, g * DK:(g + 1) * DK],
                                       gr[0:RANK, :], start=True, stop=True)
                    mm.then_inc(*filled(("z", i)))
                for t in range(TT):
                    mm = pe.transpose(iw_bank[:, t * IH:(t + 1) * IH], misc[DI:DI + IH, t * P:(t + 1) * P],
                                      ident[DI:DI + IH, DI:DI + IH])
                mm.then_inc(*filled(("iw", 0)))
                features(3)
                need("rot")
                for i in range(4):
                    bank = fill(("log0", i))
                    for c in range(2):
                        mm = pe.matmul(bank[:, c * SEQ:(c + 1) * SEQ], ts[:, T_IQ + 2 * i + c, 0:P],
                                       ikz[:, :, 0:P], start=True, stop=True)
                    mm.then_inc(*filled(("log0", i)))
                for i in range(8):
                    bank = fill(("log1", i))
                    pe.matmul(bank, ts[:, T_IQ + i, P:SEQ], ikz[:], start=True, stop=True) \
                        .then_inc(*filled(("log1", i)))

                def scores(t):
                    keys = (t + 1) * P
                    heads = 512 // keys
                    for i in range(AH // heads):
                        bank = fill((f"sc{t}", i))
                        for c in range(heads):
                            a = heads * i + c
                            mm = pe.matmul(bank[:, c * keys:(c + 1) * keys], ts[:, T_DQ + a, t * P:(t + 1) * P],
                                           ts[:, T_DK + a, 0:keys], start=True, stop=True)
                        mm.then_inc(*filled((f"sc{t}", i)))

                def transpose_probs(t):
                    need("probs", t + 1)
                    for i in range(2 * (t + 1)):
                        bank = fill((f"pt{t}", i))
                        for c in range(4):
                            a, j = (4 * i + c, 0) if t == 0 else (2 * i + c // 2, c % 2)
                            mm = pe.transpose(bank[:, c * P:(c + 1) * P], probs[:, a, j * P:(j + 1) * P], ident[:])
                        mm.then_inc(*filled((f"pt{t}", i)))

                def attend(t):
                    taken((f"pt{t}", 2 * t + 1))
                    for i in range(2):
                        bank = fill((f"pv{t}", i))
                        for c in range(4):
                            a = 4 * i + c
                            for j in range(t + 1):
                                mm = pe.matmul(bank[:, c * P:(c + 1) * P], dv[:, j, a * DH:(a + 1) * DH],
                                               ptT[:, a, j, :], start=(j == 0), stop=(j == t))
                        mm.then_inc(*filled((f"pv{t}", i)))

                straight = [2 * b for b in range(RAW)]

                def tok(j):
                    token_octet(n0 + 8 * (O_TOK + j), j % 2, A_TOK + j // 2, y, straight)

                tok(0)
                tok(1)
                scores(0)
                tok(2)
                transpose_probs(0)
                scores(1)
                tok(3)
                for j in range(2):
                    pe.wait_ge(acc_free[j], pair_free(L, j, A_TOK + 1))
                for i in range(2):
                    taken(("pt0", i))
                attend(0)
                transpose_probs(1)
                need("gla_q")
                need("gla_kinv")
                need("gla_k")
                at_bank = fill(("at", 0))
                for t in range(TT):
                    bank = fill(("kd", t))
                    for g in range(GH):
                        mm = pe.transpose(bank[:, g * DK:(g + 1) * DK], ts[:, T_GK + g, t * P:(t + 1) * P], ident[:])
                    mm.then_inc(*filled(("kd", t)))
                for n in range(NCH):
                    t, c = n // 2, n % 2
                    for g in range(GH):
                        col = (t * GH + g) * CHUNK
                        mm = pe.matmul(at_bank[c * CHUNK:(c + 1) * CHUNK, col:col + CHUNK],
                                       kinv[:, g, n * CHUNK:(n + 1) * CHUNK],
                                       ts[:, T_GQ + g, n * CHUNK:(n + 1) * CHUNK], start=True, stop=True)
                mm.then_inc(*filled(("at", 0)))
                tok(4)
                for i in range(4):
                    taken(("pt1", i))
                attend(1)
                for j in range(2):
                    pe.wait_ge(acc_free[j], pair_free(L, j, A_TOK + 2))
                for t in range(TT):
                    taken(("kd", t))
                for n in range(NCH - 1):
                    t, rows = n // 2, slice((n % 2) * CHUNK, (n % 2 + 1) * CHUNK)
                    for gp in range(2):
                        bank = fill(("ds", 2 * n + gp))
                        for c in range(2):
                            g = 2 * gp + c
                            mm = pe.matmul(bank[:, c * DV:(c + 1) * DV], kd[rows, t, g * DK:(g + 1) * DK],
                                           gv[rows, t, g * DV:(g + 1) * DV], start=True, stop=True)
                        mm.then_inc(*filled(("ds", 2 * n + gp)))
                tok(5)
                taken(("at", 0))
                need("at_masked")
                for i in range(6):
                    taken(("ds", i))
                for t in range(TT):
                    for gp in range(2):
                        bank = fill(("o", 2 * t + gp))
                        pe.sem_inc(pe_stood, 1)
                        for c in range(2):
                            g = 2 * gp + c
                            for half in range(2):
                                n = 2 * t + half
                                rows = slice(half * CHUNK, (half + 1) * CHUNK)
                                o = bank[rows, c * DV:(c + 1) * DV]
                                mm = pe.matmul(o, at_sb[rows, t, g, :], gv[rows, t, g * DV:(g + 1) * DV],
                                               start=True, stop=(n == 0))
                                if n:
                                    mm = pe.matmul(o, ts[:, T_GQ + g, n * CHUNK:(n + 1) * CHUNK],
                                                   states[:, n - 1, g, :], start=False, stop=True)
                        mm.then_inc(*filled(("o", 2 * t + gp)))
                def o_in_place(j):
                    if j == 0:
                        for i in range(2):
                            taken(("pv1", i))
                    if j == RAW // 2:
                        for i in range(4):
                            taken(("o", i))
                        for i in range(4):
                            bank = fill(("ot", i))
                            for c in range(2):
                                for t in range(TT):
                                    k = 2 * i + c
                                    mm = pe.transpose(bank[:, c * SEQ + t * P:c * SEQ + (t + 1) * P],
                                                      gg[:, t, k * P:(k + 1) * P], ident[:])
                            mm.then_inc(*filled(("ot", i)))
                    if j >= RAW // 2:
                        taken(("ot", j - RAW // 2))

                for j in range(4):
                    token_octet(n0 + 8 * (O_OUT + j), j % 2, A_OUT + j // 2, oT, OUT_ROWS,
                                None if j else o_in_place)

                def y_in_place(b):
                    norm_transposes(2, range(4) if b == 0 else range(2 * b + 2, 2 * b + 4) if b < 3 else [])
                    taken(("norm2", 2 * b))
                    taken(("norm2", 2 * b + 1))

                def up_octet(q, i, before=None):
                    feature_octet(i * 8 + q * (8 * (UP + DN)) + (n0 + 8 * O_FFN), i + q * (UP + DN // 2) + A_FFN,
                                  before)

                def quarter(q, first=0):
                    with pe.Fori(first, UP) as i:
                        up_octet(q, i)

                    def u_in_place(j):
                        pe.wait_ge(S["u_lo"], q * 8 + at("u_lo", j + 1))

                    with pe.Fori(0, DN // 2) as i:
                        for j in range(2):
                            token_octet(i * 16 + q * (8 * (UP + DN)) + (n0 + 8 * (O_FFN + UP + j)), j,
                                        i + q * (UP + DN // 2) + (A_FFN + UP), u, straight, u_in_place)

                up_octet(0, 0, y_in_place)
                quarter(0, 1)
                with pe.Fori(1, NQ) as q:
                    quarter(q)

        @block.vector
        def _(dve):
            got = dict.fromkeys(PER, 0)
            steps = [0]
            two_pi = 2 * np.pi
            c1 = 6.28125
            c2 = float(np.uint32(np.float32(two_pi - c1).view(np.uint32) & np.uint32(0xFFFFF000)).view(np.float32))
            c3 = float(np.float32(two_pi - c1 - c2))
            magic = float(1.5 * 2 ** 23)
            below_pi = 3.1415925

            def split_lo(number, slot0, n=BLK, blocks=range(QB)):
                for b in blocks:
                    dve.wait_ge(hi_done, number + (b + 1))
                    dve.tensor_tensor(lo[:, slot0 + b, 0:n], raw[:, slot0 + b, 0:n],
                                      hi[:, b, 0:n].bitcast(F32), ALU.subtract).then_inc(lo_done, 1)

            n_set = [0]

            def set_up(i):
                n_set[0] += 1
                i.then_inc(set_dve, 1)
                dve.wait_ge(set_dve, n_set[0])

            dve.wait_ge(pos_in, 16)
            dve.wait_ge(rc_in, 16)
            set_up(dve.tensor_copy(pos_f[:], pos_i[:]))
            for i in range(2):
                set_up(dve.tensor_scalar(angle[:, i], pos_f[:], rc[:, 2 * i:2 * i + 1], None, ALU.mult))
            set_up(dve.tensor_scalar(turns[:], angle[:], 1 / two_pi, magic, ALU.mult, ALU.add))
            set_up(dve.tensor_scalar(turns[:], turns[:], magic, None, ALU.subtract))
            for part in (c1, c2, c3):
                set_up(dve.scalar_tensor_tensor(angle[:], turns[:], -part, angle[:], ALU.mult, ALU.add))
            set_up(dve.tensor_scalar(angle[:], angle[:], below_pi, -below_pi, ALU.min, ALU.max))
            set_up(dve.scalar_tensor_tensor(co_angle[:], angle[:], -1.0, angle[:], ALU.mult, ALU.max))
            set_up(dve.tensor_scalar(co_angle[:], co_angle[:], -1.0, np.pi / 2, ALU.mult, ALU.add))
            assert n_set[0] == SET_DVE_ARGS, n_set
            dve.wait_ge(set_pe, 1)
            for col, n in ((0, KT), (KT, KT), (2 * KT, GH)):
                src = work[:, 0, DEPTH * col:DEPTH * (col + n)]
                at = (DEPTH + 1) * col
                dve.tensor_copy(gains_all[:, at:at + DEPTH * n], src)
                dve.tensor_copy(gains_all[:, at + DEPTH * n:at + (DEPTH + 1) * n], src[:, 0:n])
                v = dve.tensor_copy(gains[:, col:col + n], src[:, 0:n])
            set_up(v)
            assert n_set[0] == SET_DVE_GAINS, n_set
            for b in range(QB):
                dve.wait_ge(hi_done, b + 1)
                dve.tensor_tensor(used_misc(lo, b), used_misc(raw, b), used_misc(hi, b).bitcast(F32), ALU.subtract) \
                    .then_inc(lo_done, 1)
            dve.wait_ge(consts, CONSTS)
            dve.wait_ge(set_act, 2)
            for i in range(2):
                set_up(dve.tensor_scalar(rot[:, 1, i], rot[:, 1, i], rc[:, 2 * i + 1:2 * i + 2], None, ALU.mult))

            with dve.Fori(0, DEPTH) as L:
                n0 = L * (8 * OCTETS)

                def at(name, n):
                    return L * PER[name] + n

                def need(name, n=None):
                    dve.wait_ge(S[name], at(name, PER[name] if n is None else n))

                def give(name):
                    got[name] += 1
                    return S[name], 1

                def step(i):
                    steps[0] += 1
                    i.then_inc(dve_step, 1)
                    dve.wait_ge(dve_step, L * DVE_STEPS + steps[0])

                def held():
                    dve.sem_inc(dve_stood, 1)

                def split(o, half, i8=0, blocks=range(QB)):
                    split_lo(n0 + i8 + (8 * o + half * QB), half * QB, blocks=blocks)

                def split_block(o, half, b, n=BLK):
                    split_lo(n0 + (8 * o + half * QB), half * QB, n, [b])

                def ready(f):
                    b, n = BANK[f]
                    dve.wait_ge(bank_ready[b], L * USES[b] + n + 1)
                    return work[:, b, :]

                def in_sbuf(f):
                    b, n = BANK[f]
                    dve.wait_ge(bank_free[b], L * USES[b] + n + 2)

                def taken(f):
                    return bank_free[BANK[f][0]], 1

                def newton(cols, post=False):
                    ms, r0, a, r = (stat[:, i, 0:cols] for i in (1, 3, 4, 5))
                    got["r0"] += 1
                    dve.wait_ge(S["r0"], at("r0", got["r0"]))
                    step(dve.scalar_tensor_tensor(a, ms, -0.5, r0, ALU.mult, ALU.mult))
                    step(dve.tensor_tensor(a, a, r0, ALU.mult))
                    v = dve.scalar_tensor_tensor(r, a, 1.5, r0, ALU.add, ALU.mult)
                    if post:
                        v.then_inc(*give("post_rstd"))
                        dve.wait_ge(S["post_rstd"], at("post_rstd", got["post_rstd"]))
                    else:
                        step(v)

                def rstd_of(size, cols):
                    step(dve.tensor_scalar(stat[:, 1, 0:cols], stat[:, 0, 0:cols], 1.0 / size, EPS, ALU.mult, ALU.add))
                    newton(cols)

                def pre_norm(n):
                    dve.wait_ge(S["ssq"], at("ssq", n))
                    rstd_of(D, TT)
                    r = stat[:, 5, 0:TT]
                    dve.tensor_copy(pre[:, 0, :], r)
                    dve.tensor_tensor(pre[:, 1, :], r, r, ALU.mult)
                    dve.tensor_scalar(pre[:, 2, :], r, float(DH ** -0.5), None, ALU.mult).then_inc(*give("rstd"))
                    dve.wait_ge(S["rstd"], at("rstd", got["rstd"]))
                    held()

                def update(i):
                    c = slice(i * D // NORM, (i + 1) * D // NORM)
                    for t in range(TT):
                        v = dve.scalar_tensor_tensor(h[:, t, c], facc[:, t, c], stat[:, 5, t:t + 1], h[:, t, c],
                                                     ALU.mult, ALU.add)
                    v.then_inc(h_done[0], 1)

                def y_lo(i, which, g0):
                    f = (f"norm{which}", i)
                    dve.wait_ge(S["y_hi"], at("y_hi", 8 * (which - 1) + i + 1))
                    for c in range(2):
                        k = 2 * i + c
                        v = dve.scalar_tensor_tensor(
                            y[:, k, SEQ:2 * SEQ], work[:, BANK[f][0], c * SEQ:(c + 1) * SEQ],
                            gains[:, g0 + k:g0 + k + 1], y[:, k, 0:SEQ].bitcast(F32), ALU.mult, ALU.subtract)
                    v.then_inc(*taken(f))

                def mean_squares():
                    step(dve.tensor_reduce(stat[:, 4, 0:TT], stat[:, 0, :].rearrange("p (t b) -> p t b", t=TT),
                                           AX_X, ALU.add))
                    dve.tensor_scalar(stat[:, 1, 0:TT], stat[:, 4, 0:TT], 1.0 / D, EPS, ALU.mult, ALU.add) \
                        .then_inc(*give("ms"))

                def weigh(dst, src, gain):
                    return dve.tensor_tensor(dst, src, gain.unsqueeze(1).to_broadcast([P, TT, 512]), ALU.mult)

                def rope(v, table, mask, count, dst):
                    sw = swapped[0:v.shape[0], 0:v.shape[1], :] if len(v.shape) == 3 else swapped[0:v.shape[0], 0, :]
                    cos, sin = table[:, 0, :], table[:, 1, :]
                    if len(v.shape) == 3:
                        cos, sin = (x.unsqueeze(1).to_broadcast(list(v.shape)) for x in (cos, sin))
                    held()
                    dve.stream_shuffle(sw, v, mask).then_inc(S["rot"], 1)
                    dve.wait_ge(S["rot"], count(1))
                    dve.tensor_tensor(sw, sw, sin, ALU.mult).then_inc(S["rot"], 1)
                    dve.tensor_tensor(v, v, cos, ALU.mult).then_inc(S["rot"], 1)
                    dve.wait_ge(S["rot"], count(3))
                    for d in dst[:-1]:
                        dve.tensor_tensor(d, v, sw, ALU.add)
                    dve.tensor_tensor(dst[-1], v, sw, ALU.add).then_inc(S["rot"], 1)
                    dve.wait_ge(S["rot"], count(4))

                need("gr_hi")
                dve.tensor_tensor(gr_lo[:], w_gr[:], gr_hi[:].bitcast(F32), ALU.subtract).then_inc(*give("gr_lo"))
                for i in range(NORM):
                    if i >= NORM - QB:
                        split_block(0, 1, i - (NORM - QB), 2 * MISC_W)
                    y_lo(i, 1, 0)
                for b in range(QB - 1):
                    split_block(O_T, 0, b)
                for i, (rows, dst) in enumerate(((MISC_W, misc), (RANK, gr))):
                    dve.wait_ge(S["half"], at("half", i + 1))
                    v = dve.tensor_tensor(dst[0:rows, :], acc[0:rows, 2 + i, 0:SEQ], scr[0:rows, 0, i, :], ALU.add)
                v.then_inc(acc_free[1], 1)
                split_block(O_T, 0, QB - 1)

                def features(g):
                    with dve.Fori(0, 2) as i:
                        for half in range(2):
                            split(O_T + 2 * g + half, 1 - half, i * 8)
                            dve.wait_ge(S["half"], i * 2 + at("half", 3 + 4 * g + half))
                            v, dst = fresh[:, half], ts[:, bass.ds(i * 4 + (8 * g + 2 * half), 2), :]
                            dve.tensor_tensor(v, acc[:, 2 * half:2 * half + 2, 0:SEQ], scr[:, half], ALU.add) \
                                .then_inc(acc_free[half], 1)
                            dve.wait_ge(acc_free[half], i + pair_free(L, half, A_T + 2 * g + 1))
                            count = lambda n: i * 8 + at("rot", 16 * g + 4 * half + n)
                            if g == 0:
                                rope(v, rot_i, swap_mask(8), count, [dst])
                            elif g == 1:
                                rope(v, rot_a, swap_mask(16), count, [dst])
                            elif g == 2:
                                rope(v, rot_k, swap_mask(16), count, [dst])
                            else:
                                dve.tensor_tensor(dst, v, rb[:].unsqueeze(1).to_broadcast([P, 2, SEQ]), ALU.mult)

                features(0)
                pre_norm(S_PRE)
                features(1)
                dve.tensor_copy(rb[:], ready(("rb", 0))[:, 0:SEQ]).then_inc(*taken(("rb", 0)))
                in_sbuf(("rb", 0))
                step(dve.tensor_tensor(rot_k[:], rot_a[:], rb[:].unsqueeze(1).to_broadcast([P, 2, SEQ]), ALU.mult))
                dve.tensor_tensor(misc[0:MISC_W, :], misc[0:MISC_W, :], rb[0:MISC_W, :], ALU.mult)
                dve.tensor_tensor(gr[0:RANK, :], gr[0:RANK, :], rb[0:RANK, :], ALU.mult).then_inc(*give("scaled"))
                need("scaled")
                held()
                features(2)
                bank = ready(("iw", 0))
                for t in range(TT):
                    v = dve.tensor_scalar(iw[:, t, :], bank[:, t * IH:(t + 1) * IH], pre[:, 0, t:t + 1],
                                          float(IH ** -0.5 * DI ** -0.5), ALU.mult, ALU.mult)
                v.then_inc(*taken(("iw", 0)))
                in_sbuf(("z", 0))
                in_sbuf(("z", 1))
                dve.scalar_tensor_tensor(zb[:], za[:], -1.0, za[:], ALU.mult, ALU.max).then_inc(*give("zabs"))
                rope(misc[0:DI, :], rot_i[0:DI], swap_mask(8),
                     lambda n: at("rot", 48 + n), [ikz[0:DI, 0, :], ikz[DI:2 * DI, 1, :]])
                held()
                features(3)

                def sum_heads(t, i, n):
                    keys = (t + 1) * P
                    heads = 512 // keys
                    in_sbuf((f"log{t}", i))
                    for c in range(heads):
                        head = heads * i + c
                        r = relus[:, n % BANKS, c * keys:(c + 1) * keys]
                        s = score[:, t, 0:keys]
                        w = iw[:, t, head:head + 1]
                        if head == 0:
                            v = dve.tensor_scalar(s, r, w, None, ALU.mult)
                        else:
                            v = dve.scalar_tensor_tensor(s, r, w, s, ALU.mult, ALU.add)
                        if c < heads - 1:
                            step(v)
                    v.then_inc(*give("relu_used"))
                    dve.wait_ge(S["relu_used"], at("relu_used", n + 1))

                def top_k(rounds):
                    s = [score[:, t, 0:(t + 1) * P] for t in range(TT)]
                    for _ in range(rounds):
                        held()
                        for t in range(TT - 1):
                            dve.max(top8[:, t, :], s[t])
                        step(dve.max(top8[:, TT - 1, :], s[TT - 1]))
                        held()
                        for t in range(TT - 1):
                            dve.match_replace(s[t], top8[:, t, :], s[t], TAKEN)
                        step(dve.match_replace(s[TT - 1], top8[:, TT - 1, :], s[TT - 1], TAKEN))

                def bias():
                    for t in range(TT):
                        s = score[:, t, 0:(t + 1) * P]
                        dve.tensor_scalar(s, s, 10 * NEG, NEG, ALU.is_gt, ALU.mult).then_inc(*give("masked"))

                for t in range(TT):
                    for i in range(4 * (t + 1)):
                        sum_heads(t, i, 4 * t + i)

                def softmax_in(t):
                    keys = (t + 1) * P
                    heads = 512 // keys
                    need("allowed", t + 1)
                    bias = score[:, t, 0:keys].unsqueeze(1).to_broadcast([P, heads, keys])
                    for i in range(AH // heads):
                        f = (f"sc{t}", i)
                        bank = ready(f).rearrange("p (a q) -> p a q", q=keys)
                        dve.scalar_tensor_tensor(probs[:, heads * i:heads * (i + 1), 0:keys], bank, pre[:, 2, t:t + 1],
                                                 bias, ALU.mult, ALU.add).then_inc(*taken(f))
                        in_sbuf(f)
                    step(dve.tensor_reduce(smax[:, 0, :], probs[:, :, 0:keys], AX_X, ALU.max))
                    dve.tensor_scalar(smax[:, 0, :], smax[:, 0, :], -1.0, None, ALU.mult).then_inc(*give("negmax"))

                def softmax_out(t):
                    keys = (t + 1) * P
                    need("expd", t + 1)
                    step(dve.reciprocal(smax[:, 2, :], smax[:, 1, :]))
                    v = probs[:, :, 0:keys]
                    dve.tensor_tensor(v, v, smax[:, 2, :].unsqueeze(2).to_broadcast([P, AH, keys]), ALU.mult) \
                        .then_inc(*give("probs"))

                def attended_lo(t):
                    for i in range(2):
                        f, k0 = (f"pv{t}", i), KT // 2 + 4 * i
                        need("pv_hi", 2 * t + i + 1)
                        dve.tensor_tensor(oT[:, k0:k0 + 4, SEQ + t * P:SEQ + (t + 1) * P],
                                          work[:, BANK[f][0], :].rearrange("p (a q) -> p a q", q=P),
                                          oT[:, k0:k0 + 4, t * P:(t + 1) * P].bitcast(F32), ALU.subtract) \
                            .then_inc(*taken(f))

                def gate(j):
                    need("gate_e", j + 1)
                    e, g = scr_gate[:, :, j, :], gg[:, :, 512 * j:512 * j + 512]
                    step(dve.tensor_tensor(g, g, e, ALU.mult))
                    if j == 0:
                        dve.wait_ge(gnorm_in, L * 16 + 16)
                    for t in range(TT):
                        v = g[:, t, :].rearrange("p (g c) -> p g c", c=DV)
                        step(dve.tensor_tensor(v, v, gnorm[:].unsqueeze(1).to_broadcast([P, 2, DV]), ALU.mult))

                split(O_TOK, 1)
                need("causal")
                top_k(TOPK // 16)
                split(O_TOK + 1, 0)
                top_k(TOPK // 8 - TOPK // 16)
                bias()
                split(O_TOK + 1, 1)
                split(O_TOK + 2, 0)
                softmax_in(0)
                need("zl")
                step(dve.scalar_tensor_tensor(za[:], za[:], 0.0, zb[:], ALU.min, ALU.subtract))
                for g in range(GH):
                    v = dve.tensor_tensor_scan(zb[:, g, :], within[:], za[:, g, :], 0.0, ALU.mult, ALU.add)
                v.then_inc(*give("zsc"))
                need("zsc")
                split(O_TOK + 2, 1)
                softmax_out(0)
                split(O_TOK + 3, 0)
                need("eb")
                v = ts[:, T_GQ:T_GQ + GH, :]
                dve.scalar_tensor_tensor(v, v, float(DK ** -0.5), za[:], ALU.mult, ALU.mult).then_inc(*give("gla_q"))
                zc = za[:].rearrange("p g (n c) -> p (g n) c", c=CHUNK)
                step(dve.tensor_copy(decay[:].rearrange("p g n -> p (g n)"), zc[:, :, CHUNK - 1]))
                need("gla_q")
                bc = zb[:].rearrange("p g (n c) -> p (g n) c", c=CHUNK)
                dve.tensor_tensor(zc, bc, bc[:, :, CHUNK - 1:CHUNK].to_broadcast([P, GH * NCH, CHUNK]), ALU.subtract) \
                    .then_inc(*give("edin"))
                need("enb")
                k = ts[:, T_GK:T_GK + GH, :]
                dve.tensor_tensor(kinv[:], kinv[:], k, ALU.mult).then_inc(*give("gla_kinv"))
                softmax_in(1)
                split(O_TOK + 3, 1)
                softmax_out(1)
                need("gla_kinv")
                need("edec")
                dve.tensor_tensor(k, k, za[:], ALU.mult).then_inc(*give("gla_k"))
                split(O_TOK + 4, 0)
                attended_lo(0)
                split(O_TOK + 4, 1)
                split(O_TOK + 5, 0)
                attended_lo(1)
                for n in range(NCH - 1):
                    for gp in range(2):
                        f = ("ds", 2 * n + gp)
                        bank = ready(f)
                        if n == 0:
                            v = dve.tensor_copy(states[:, 0, 2 * gp:2 * gp + 2, :].rearrange("p g c -> p (g c)"), bank)
                        else:
                            in_sbuf(("ds", 2 * (n - 1) + gp))
                            for c in range(2):
                                g = 2 * gp + c
                                v = dve.scalar_tensor_tensor(states[:, n, g, :], states[:, n - 1, g, :],
                                                             decay[:, g, n:n + 1], bank[:, c * DV:(c + 1) * DV],
                                                             ALU.mult, ALU.add)
                        v.then_inc(*taken(f))
                gate(0)
                split(O_TOK + 5, 1)
                split(O_OUT, 0)
                gate(1)
                need("ossq")
                rstd_of(DV, TT * GH)
                for t in range(TT):
                    for gp in range(2):
                        f = ("o", 2 * t + gp)
                        for c in range(2):
                            g = 2 * gp + c
                            v = gg[:, t, g * DV:(g + 1) * DV]
                            i = dve.scalar_tensor_tensor(v, work[:, BANK[f][0], c * DV:(c + 1) * DV],
                                                         stat[:, 5, t * GH + g:t * GH + g + 1], v, ALU.mult, ALU.mult)
                        i.then_inc(*taken(f))
                for b in range(QB - 1):
                    split_block(O_OUT, 1, b)
                for i in range(4):
                    f = ("ot", i)
                    need("ot_hi", i + 1)
                    dve.tensor_tensor(oT[:, 2 * i:2 * i + 2, SEQ:2 * SEQ],
                                      work[:, BANK[f][0], :].rearrange("p (k q) -> p k q", q=SEQ),
                                      oT[:, 2 * i:2 * i + 2, 0:SEQ].bitcast(F32), ALU.subtract).then_inc(*taken(f))
                split_block(O_OUT, 1, QB - 1)

                def weigh_block(j):
                    c = slice(512 * j, 512 * (j + 1))
                    weigh(facc[:, :, c], acc[:, 2 * (j % 2):2 * (j % 2) + 2, :], gpost[:, c]) \
                        .then_inc(acc_free[j % 2], 1)
                    dve.wait_ge(acc_free[j % 2], pair_free(L, j % 2, A_OUT + j // 2) + 1)

                for j in range(4):
                    if j:
                        split(O_OUT + j, 1)
                    for b in range(QB if j < 3 else QB - 1):
                        split_block(O_OUT + j + 1, 0, b)
                    need("ssq", S_OUT + j)
                    if j == 0:
                        dve.wait_ge(gpost_in, L * 32 + 16)
                    if j == 3:
                        mean_squares()
                        newton(TT, post=True)
                    if j < 3:
                        weigh_block(j)

                update(0)
                update(2)
                weigh_block(3)
                update(4)
                for i in range(NORM):
                    y_lo(i, 2, KT)
                    if i == 0:
                        update(6)
                    if i == 4:
                        split_block(O_FFN, 0, QB - 1)

                def down(q, i, j, first=False):
                    i8 = (i * 2 + q * (UP + DN)) * 8
                    o = O_FFN + UP + j
                    split(o, 1, i8)
                    split(o + 1, 0, i8, blocks=range(QB - 1))
                    dve.wait_ge(block_done, done(i8 + (n0 + (8 * o + RAW - 1))))
                    for t in range(TT):
                        a, r2 = acc[:, 2 * j + t, :], pre[:, 1, t:t + 1]
                        v = facc[:, t, bass.ds(i * 1024 + j * 512, 512)]
                        if first:
                            v = dve.tensor_scalar(v, a, r2, None, ALU.mult)
                        else:
                            v = dve.scalar_tensor_tensor(v, a, r2, v, ALU.mult, ALU.add)
                    v.then_inc(acc_free[j], 1)
                    split(o + 1, 0, i8, blocks=[QB - 1])

                def quarter(q, first=False, last=False):
                    with dve.Fori(0, UP) as i:
                        i8 = (i + q * (UP + DN)) * 8
                        for half in range(2):
                            split(O_FFN + half, 1 - half, i8)
                            g = i * 2 + q * 8
                            dve.wait_ge(S["half"], g + at("half", 3 + 16 + half))
                            dve.tensor_tensor(u2[:, half], acc[:, 2 * half:2 * half + 2, 0:SEQ], scr[:, half], ALU.add) \
                                .then_inc(acc_free[half], 1)
                            dve.wait_ge(acc_free[half], i + q * (UP + DN // 2) + pair_free(L, half, A_FFN + 1))
                            dve.scalar_tensor_tensor(u2[:, half], u2[:, half], 0.0, u2[:, half], ALU.max, ALU.mult) \
                                .then_inc(S["squared"], 1)
                            dve.wait_ge(S["u_hi"], g + at("u_hi", 1 + half))
                            ut = bass.ds(i * 4 + 2 * half, 2)
                            dve.tensor_tensor(u[:, ut, SEQ:2 * SEQ], u2[:, half], u[:, ut, 0:SEQ].bitcast(F32),
                                              ALU.subtract).then_inc(S["u_lo"], 1)
                    if first:
                        pre_norm(S_PRE2)
                    if not last:
                        with dve.Fori(0, DN // 2) as i:
                            for j in range(2):
                                down(q, i, j, first)

                quarter(0, first=True)
                with dve.Fori(1, NQ - 1) as q:
                    quarter(q)
                quarter(NQ - 1, last=True)
                dve.wait_ge(gpost_in, L * 32 + 32)
                for j in range(DN):
                    down(NQ - 1, j // 2, j % 2)
                    need("ssq", S_DOWN + j)
                    if j == DN - 1:
                        mean_squares()
                    c = slice(512 * j, 512 * (j + 1))
                    if j < DN - 1:
                        weigh(facc[:, :, c], facc[:, :, c], gpost[:, c]).then_inc(weighed, 1)

                for col, n in ((0, KT), (KT, KT), (2 * KT, GH)):
                    v = dve.tensor_copy(gains[:, col:col + n], gains_all[:, bass.ds(L * n + ((DEPTH + 1) * col + n), n)])
                step(v)
                newton(TT, post=True)
                dve.wait_ge(weighed, L * DN + (DN - 1))
                update(0)
                update(2)
                weigh(facc[:, :, c], facc[:, :, c], gpost[:, c]).then_inc(weighed, 1)
                dve.wait_ge(weighed, L * DN + DN)
                update(4)
                update(6)
            assert steps[0] == DVE_STEPS, steps
            for n in ("ms", "r0", "rstd", "zabs", "scaled", "zsc", "edin", "gla_q", "gla_kinv", "gla_k",
                      "relu_used", "masked", "negmax", "probs", "post_rstd", "gr_lo"):
                assert got[n] == PER[n], (n, got[n])


_INS = ["x", "positions", "norm_mix_pre", "w_in", "gla_wa2", "gla_ba", "gla_norm", "w_out", "norm_mix_post",
        "norm_ffn_pre", "w_up", "w_down", "norm_ffn_post"]


def kernel(**inputs):
    import concourse.bacc as bacc
    from concourse.bass_utils import run_bass_kernel_spmd

    nc = bacc.Bacc("TRN2", target_bir_lowering=False, num_devices=1)
    arrays = {f"in_{n}": np.ascontiguousarray(inputs[n]) for n in _INS}
    arrays["in_rope_constants"] = rope_constants()
    args = [nc.dram_tensor(n, a.shape, mybir.dt.from_np(a.dtype), kind="ExternalInput").ap()
            for n, a in arrays.items()]
    args.append(nc.dram_tensor("out", (1, SEQ, D), F32, kind="ExternalOutput").ap())
    trunk(nc, *args)
    return run_bass_kernel_spmd(nc, [arrays], core_ids=[0]).results[0]["out"]
```
